# Optimizing a Trainium2 kernel written in Bass

```python
import math
import jax
import jax.numpy as jnp
from jax import lax
import numpy as np

D_MODEL = 1024
BATCH = 1
SEQ = 512
DEPTH = 2

GRID_W = 64
CTX_LEN = 256
HEAD_DIM = 64
ROPE_BASE = 10000.0
NORM_EPS = 1e-6
BLOCK = 128

A_HEADS = 8
A_KV_HEADS = 2
A_GROUP = A_HEADS // A_KV_HEADS
A_WINDOW = 128
A_WIDTH = A_HEADS * HEAD_DIM
A_KV_WIDTH = A_KV_HEADS * HEAD_DIM

B_INNER = D_MODEL
B_HEAD_DIM = 64
B_HEADS = B_INNER // B_HEAD_DIM
B_GROUPS = 2
B_HPG = B_HEADS // B_GROUPS
B_STATE = 128
B_CONV = 5
B_CHUNK = 128
B_XBC = B_INNER + 2 * B_GROUPS * B_STATE

C_HEADS = D_MODEL // (2 * HEAD_DIM)
C_VDIM = 2 * HEAD_DIM
C_WIDTH = C_HEADS * C_VDIM

EVEN_SPLITS = (A_WIDTH, A_KV_WIDTH, A_KV_WIDTH, A_WIDTH, B_INNER, B_XBC, 2 * B_HEADS)
EVEN_IN = A_WIDTH + A_KV_WIDTH + A_KV_WIDTH + A_WIDTH + B_INNER + B_XBC + 2 * B_HEADS
EVEN_MIX = A_WIDTH + B_INNER
ODD_IN = 4 * C_WIDTH
N_EVEN = (DEPTH + 1) // 2
N_ODD = DEPTH // 2

kernel_name = 'hybrid_swa_ssd_diffattn_prefix_trunk'

def rms_norm(x, w):
    xf = x.astype(jnp.float32)
    y = xf * lax.rsqrt(jnp.mean(xf * xf, axis=-1, keepdims=True) + NORM_EPS)
    return (y * w.astype(jnp.float32)).astype(x.dtype)

def axial_rope(length, dtype):
    rows = length // GRID_W
    row = jnp.repeat(jnp.arange(rows), GRID_W).astype(jnp.float32)
    col = jnp.tile(jnp.arange(GRID_W), rows).astype(jnp.float32)
    n_freq = HEAD_DIM // 4
    inv_freq = ROPE_BASE ** (-jnp.arange(n_freq, dtype=jnp.float32) / n_freq)
    ang_r = row[:, None] * inv_freq
    ang_c = col[:, None] * inv_freq
    ang = jnp.concatenate([ang_r, ang_r, ang_c, ang_c], axis=-1)
    return jnp.cos(ang).astype(dtype), jnp.sin(ang).astype(dtype)

def apply_rope(x, cos, sin):
    shape = (1, x.shape[1]) + (1,) * (x.ndim - 3) + (HEAD_DIM,)
    x1, x2, x3, x4 = jnp.split(x, 4, axis=-1)
    x_rot = jnp.concatenate([-x2, x1, -x4, x3], axis=-1)
    return x * cos.reshape(shape) + x_rot * sin.reshape(shape)

def sink_softmax(parts, sink):
    m = sink
    for s in parts:
        m = jnp.maximum(m, jnp.max(s, axis=-1, keepdims=True))
    exps = [jnp.exp(s - m) for s in parts]
    denom = jnp.exp(sink - m)
    for e in exps:
        denom = denom + jnp.sum(e, axis=-1, keepdims=True)
    return [e / denom for e in exps]

def window_attention(q, k, v, ck, cv, sink):
    bsz, length = q.shape[:2]
    n_blocks = length // BLOCK
    scale = HEAD_DIM ** -0.5
    qb = q.reshape(bsz, n_blocks, BLOCK, A_KV_HEADS, A_GROUP, HEAD_DIM)

    def band(t):
        tb = jnp.pad(t.reshape(bsz, n_blocks, BLOCK, A_KV_HEADS, HEAD_DIM), ((0, 0), (1, 1), (0, 0), (0, 0), (0, 0)))
        return jnp.concatenate([tb[:, :-2], tb[:, 1:-1], tb[:, 2:]], axis=2)

    kw, vw = band(k), band(v)
    q_pos = jnp.arange(length).reshape(n_blocks, BLOCK)
    k_pos = jnp.arange(n_blocks)[:, None] * BLOCK + jnp.arange(-BLOCK, 2 * BLOCK)[None, :]
    valid = ((jnp.abs(q_pos[:, :, None] - k_pos[:, None, :]) <= A_WINDOW)
             & (k_pos[:, None, :] >= 0) & (k_pos[:, None, :] < length))
    s_loc = jnp.einsum('bnqhgd,bnkhd->bnhgqk', qb, kw).astype(jnp.float32) * scale
    s_loc = jnp.where(valid[None, :, None, None], s_loc, -jnp.inf)
    s_ctx = jnp.einsum('bnqhgd,bchd->bnhgqc', qb, ck).astype(jnp.float32) * scale
    p_loc, p_ctx = sink_softmax([s_loc, s_ctx], sink[None, None, :, :, None, None])
    out = (jnp.einsum('bnhgqk,bnkhd->bnqhgd', p_loc.astype(vw.dtype), vw)
           + jnp.einsum('bnhgqc,bchd->bnqhgd', p_ctx.astype(cv.dtype), cv))
    return out.reshape(bsz, length, A_KV_HEADS, A_GROUP, HEAD_DIM)

def context_attention(q, k, v, sink):
    s = jnp.einsum('bqhgd,bkhd->bhgqk', q, k).astype(jnp.float32) * HEAD_DIM ** -0.5
    (p,) = sink_softmax([s], sink[None, :, :, None, None])
    return jnp.einsum('bhgqk,bkhd->bqhgd', p.astype(v.dtype), v)

def depthwise_conv(u, w, b):
    out = lax.conv_general_dilated(u, w[:, None, :].astype(u.dtype), window_strides=(1,),
                                   padding=[(B_CONV // 2, B_CONV // 2)],
                                   dimension_numbers=('NWC', 'WIO', 'NWC'),
                                   feature_group_count=u.shape[-1])
    return out + b.astype(u.dtype)

def ssd_scan(x, dt, a, b, c, h0):
    bsz, length = x.shape[:2]
    nc = length // B_CHUNK
    x = x.reshape(bsz, nc, B_CHUNK, B_GROUPS, B_HPG, B_HEAD_DIM)
    dt = dt.reshape(bsz, nc, B_CHUNK, B_GROUPS, B_HPG)
    b = b.reshape(bsz, nc, B_CHUNK, B_GROUPS, B_STATE)
    c = c.reshape(bsz, nc, B_CHUNK, B_GROUPS, B_STATE)
    la = jnp.cumsum(dt * a, axis=2)
    xdt = x * dt[..., None]
    lower = jnp.tril(jnp.ones((B_CHUNK, B_CHUNK), dtype=bool))
    seg = la[:, :, :, None] - la[:, :, None]
    decay = jnp.exp(jnp.where(lower[None, None, :, :, None, None], seg, -jnp.inf))
    cb = jnp.einsum('bctgn,bcsgn->bctsg', c, b)
    y_intra = jnp.einsum('bctsg,bctsgh,bcsghp->bctghp', cb, decay, xdt)
    w_end = jnp.exp(la[:, :, -1:] - la)
    states = jnp.einsum('bcsgn,bcsgh,bcsghp->bcghpn', b, w_end, xdt)
    chunk_decay = jnp.exp(la[:, :, -1])

    def step(h, inp):
        s_c, d_c = inp
        return h * d_c[..., None, None] + s_c, h

    h_last, h_in = lax.scan(step, h0, (jnp.moveaxis(states, 1, 0), jnp.moveaxis(chunk_decay, 1, 0)))
    h_in = jnp.moveaxis(h_in, 0, 1)
    y_inter = jnp.einsum('bctgn,bcghpn,bctgh->bctghp', c, h_in, jnp.exp(la))
    return (y_intra + y_inter).reshape(bsz, length, B_GROUPS, B_HPG, B_HEAD_DIM), h_last

def flip_seq(t):
    return jnp.flip(t, axis=1)

def bidir_ssd(xs, dt, a, bm, cm, d_skip, h0_f, h0_b):
    y_f, h_f = ssd_scan(xs, dt[:, :, 0], a[0], bm, cm, h0_f)
    y_b, h_b = ssd_scan(flip_seq(xs), flip_seq(dt[:, :, 1]), a[1], flip_seq(bm), flip_seq(cm), h0_b)
    return y_f + flip_seq(y_b) + d_skip[:, :, None] * xs, h_f, h_b

def attn_ssd_layer(hx, hc, w_in, w_out, q_norm, k_norm, sink, conv_w, conv_b, dt_bias, a_log, d_skip,
                   ssm_norm, need_ctx):
    split_at = [int(s) for s in np.cumsum(EVEN_SPLITS)[:-1]]
    sink = sink.astype(jnp.float32).reshape(A_KV_HEADS, A_GROUP)
    a = -jnp.exp(a_log.astype(jnp.float32)).reshape(2, B_GROUPS, B_HPG)
    d_skip = d_skip.astype(jnp.float32).reshape(B_GROUPS, B_HPG)
    dt_bias = dt_bias.astype(jnp.float32).reshape(2, B_GROUPS, B_HPG)

    def branch_inputs(h):
        bsz, length = h.shape[:2]
        q, k, v, ga, z, xbc, dt = jnp.split(h @ w_in, split_at, axis=-1)
        q = rms_norm(q.reshape(bsz, length, A_KV_HEADS, A_GROUP, HEAD_DIM), q_norm)
        k = rms_norm(k.reshape(bsz, length, A_KV_HEADS, HEAD_DIM), k_norm)
        v = v.reshape(bsz, length, A_KV_HEADS, HEAD_DIM)
        xbc = jax.nn.silu(depthwise_conv(xbc, conv_w, conv_b)).astype(jnp.float32)
        xs, bm, cm = jnp.split(xbc, [B_INNER, B_INNER + B_GROUPS * B_STATE], axis=-1)
        xs = xs.reshape(bsz, length, B_GROUPS, B_HPG, B_HEAD_DIM)
        bm = bm.reshape(bsz, length, B_GROUPS, B_STATE)
        cm = cm.reshape(bsz, length, B_GROUPS, B_STATE)
        dt = jax.nn.softplus(dt.astype(jnp.float32).reshape(bsz, length, 2, B_GROUPS, B_HPG) + dt_bias)
        return q, k, v, ga, z, xs, dt, bm, cm

    def ssm_output(xs, dt, bm, cm, z, h0_f, h0_b):
        y, h_f, h_b = bidir_ssd(xs, dt, a, bm, cm, d_skip, h0_f, h0_b)
        y = y.reshape(z.shape).astype(z.dtype) * jax.nn.silu(z)
        return rms_norm(y, ssm_norm), h_f, h_b

    def merge(att, ga, y):
        att = att.reshape(ga.shape) * jax.nn.silu(ga)
        return jnp.concatenate([att, y], axis=-1) @ w_out

    bsz, length = hx.shape[:2]
    cq, ck, cv, cga, cz, cxs, cdt, cbm, ccm = branch_inputs(hc)
    h0 = jnp.zeros((bsz, B_GROUPS, B_HPG, B_HEAD_DIM, B_STATE), jnp.float32)
    y_c, h_f, h_b = ssm_output(cxs, cdt, cbm, ccm, cz, h0, h0)
    q, k, v, ga, z, xs, dt, bm, cm = branch_inputs(hx)
    cos, sin = axial_rope(length, hx.dtype)
    att = window_attention(apply_rope(q, cos, sin), apply_rope(k, cos, sin), v, ck, cv, sink)
    y, _, _ = ssm_output(xs, dt, bm, cm, z, h_f, h_b)
    out_x = merge(att, ga, y)
    out_c = merge(context_attention(cq, ck, cv, sink), cga, y_c) if need_ctx else None
    return out_x, out_c

def diff_attend(q, k, v, lam):
    s = jnp.einsum('bqhcd,bkhcd->bchqk', q, k).astype(jnp.float32) * HEAD_DIM ** -0.5
    p = jax.nn.softmax(s, axis=-1)
    a = (p[:, 0] - lam * p[:, 1]).astype(v.dtype)
    return jnp.einsum('bhqk,bkhv->bqhv', a, v)

def diff_attn_layer(hx, hc, w_in, w_out, q_norm, k_norm, lam_params, head_norm, lambda_init, need_ctx):
    lp = lam_params.astype(jnp.float32)
    lam = jnp.exp(jnp.sum(lp[0] * lp[1])) - jnp.exp(jnp.sum(lp[2] * lp[3])) + lambda_init

    def branch_inputs(h):
        bsz, length = h.shape[:2]
        q, k, v, g = jnp.split(h @ w_in, 4, axis=-1)
        q = rms_norm(q.reshape(bsz, length, C_HEADS, 2, HEAD_DIM), q_norm)
        k = rms_norm(k.reshape(bsz, length, C_HEADS, 2, HEAD_DIM), k_norm)
        v = v.reshape(bsz, length, C_HEADS, C_VDIM)
        return q, k, v, g

    def finish(o, g):
        o = rms_norm(o, head_norm) * (1.0 - lambda_init)
        return (o.reshape(g.shape) * jax.nn.silu(g)) @ w_out

    bsz, length = hx.shape[:2]
    cq, ck, cv, cg = branch_inputs(hc)
    q, k, v, g = branch_inputs(hx)
    cos, sin = axial_rope(length, hx.dtype)
    q = apply_rope(q, cos, sin)
    k_all = jnp.concatenate([ck, apply_rope(k, cos, sin)], axis=1)
    v_all = jnp.concatenate([cv, v], axis=1)
    n_blocks = length // BLOCK
    q_blocks = jnp.moveaxis(q.reshape(bsz, n_blocks, BLOCK, C_HEADS, 2, HEAD_DIM), 1, 0)
    o = lax.map(lambda qb: diff_attend(qb, k_all, v_all, lam), q_blocks)
    o = jnp.moveaxis(o, 0, 1).reshape(bsz, length, C_HEADS, C_VDIM)
    out_x = finish(o, g)
    out_c = finish(diff_attend(cq, ck, cv, lam), cg) if need_ctx else None
    return out_x, out_c

def setup_inputs(seed: int = 0) -> dict:
    key = jax.random.key(seed)
    ks = jax.random.split(key, 24)
    f32 = jnp.float32

    def normal(k, shape, scale):
        return jax.random.normal(k, shape, f32) * scale

    def gain(k, shape, noise=0.01):
        return 1.0 + noise * jax.random.normal(k, shape, f32)

    dt0 = jnp.exp(jax.random.uniform(ks[14], (N_EVEN, 2, B_HEADS), f32, math.log(1e-3), math.log(1e-1)))
    return {
        'x': normal(ks[0], (BATCH, SEQ, D_MODEL), 1.0),
        'c': normal(ks[1], (BATCH, D_MODEL), 1.0),
        'ctx': normal(ks[2], (BATCH, CTX_LEN, D_MODEL), 1.0),
        'c_ctx': normal(ks[3], (D_MODEL,), 1.0),
        'mod_w': normal(ks[4], (DEPTH, D_MODEL, 3 * D_MODEL), 0.5 * D_MODEL ** -0.5),
        'mod_b': normal(ks[5], (DEPTH, 3 * D_MODEL), 0.01),
        'norm_w': gain(ks[6], (DEPTH, D_MODEL)),
        'ev_w_in': normal(ks[7], (N_EVEN, D_MODEL, EVEN_IN), D_MODEL ** -0.5),
        'ev_w_out': normal(ks[8], (N_EVEN, EVEN_MIX, D_MODEL), EVEN_MIX ** -0.5),
        'ev_q_norm': gain(ks[9], (N_EVEN, HEAD_DIM)),
        'ev_k_norm': gain(ks[10], (N_EVEN, HEAD_DIM)),
        'ev_sink': normal(ks[11], (N_EVEN, A_HEADS), 0.5),
        'ev_conv_w': normal(ks[12], (N_EVEN, B_CONV, B_XBC), B_CONV ** -0.5),
        'ev_conv_b': normal(ks[13], (N_EVEN, B_XBC), 0.01),
        'ev_dt_bias': dt0 + jnp.log(-jnp.expm1(-dt0)),
        'ev_a_log': jnp.log(jax.random.uniform(ks[15], (N_EVEN, 2, B_HEADS), f32, 1.0, 16.0)),
        'ev_d_skip': gain(ks[16], (N_EVEN, B_HEADS), 0.1),
        'ev_ssm_norm': gain(ks[17], (N_EVEN, B_INNER)),
        'od_w_in': normal(ks[18], (N_ODD, D_MODEL, ODD_IN), D_MODEL ** -0.5),
        'od_w_out': normal(ks[19], (N_ODD, C_WIDTH, D_MODEL), C_WIDTH ** -0.5),
        'od_q_norm': gain(ks[20], (N_ODD, HEAD_DIM)),
        'od_k_norm': gain(ks[21], (N_ODD, HEAD_DIM)),
        'od_lambda': normal(ks[22], (N_ODD, 4, HEAD_DIM), 0.1),
        'od_head_norm': gain(ks[23], (N_ODD, C_VDIM)),
    }

def reference(x, c, ctx, c_ctx, mod_w, mod_b, norm_w, ev_w_in, ev_w_out, ev_q_norm, ev_k_norm, ev_sink,
              ev_conv_w, ev_conv_b, ev_dt_bias, ev_a_log, ev_d_skip, ev_ssm_norm, od_w_in, od_w_out,
              od_q_norm, od_k_norm, od_lambda, od_head_norm):
    for li in range(DEPTH):
        need_ctx = li < DEPTH - 1
        shift, scale, gate = jnp.split(jax.nn.silu(c) @ mod_w[li] + mod_b[li], 3, axis=-1)
        shift_c, scale_c, gate_c = jnp.split(jax.nn.silu(c_ctx) @ mod_w[li] + mod_b[li], 3, axis=-1)
        hx = rms_norm(x, norm_w[li]) * (1.0 + scale[:, None]) + shift[:, None]
        hc = rms_norm(ctx, norm_w[li]) * (1.0 + scale_c) + shift_c
        j = li // 2
        if li % 2 == 0:
            out_x, out_c = attn_ssd_layer(hx, hc, ev_w_in[j], ev_w_out[j], ev_q_norm[j], ev_k_norm[j], ev_sink[j],
                                          ev_conv_w[j], ev_conv_b[j], ev_dt_bias[j], ev_a_log[j], ev_d_skip[j],
                                          ev_ssm_norm[j], need_ctx)
        else:
            lambda_init = 0.8 - 0.6 * math.exp(-0.3 * li)
            out_x, out_c = diff_attn_layer(hx, hc, od_w_in[j], od_w_out[j], od_q_norm[j], od_k_norm[j],
                                           od_lambda[j], od_head_norm[j], lambda_init, need_ctx)
        x = x + gate[:, None] * out_x
        if need_ctx:
            ctx = ctx + gate_c * out_c
    return x


_drawn_inputs = setup_inputs


def setup_inputs(seed=0):
    import zlib

    import numpy as np

    out = dict(_drawn_inputs(seed))
    spreads = {}
    factors = {'mod_b': 4.819,
     'norm_w': 8.0,
     'ev_q_norm': 8.0,
     'ev_k_norm': 8.0,
     'ev_sink': 8.0,
     'ev_conv_b': 8.0,
     'ev_d_skip': 43.856,
     'ev_ssm_norm': 21.416,
     'od_q_norm': 8.0,
     'od_k_norm': 8.0,
     'od_lambda': 8.0,
     'od_head_norm': 56.886}
    for name, (base, spread) in spreads.items():
        noise = np.random.default_rng([zlib.crc32(name.encode()), seed]).standard_normal(out[name].shape)
        drawn = base * np.exp(spread * noise) if base else spread * noise
        out[name] = jnp.asarray(drawn.astype(out[name].dtype))
    for name, factor in factors.items():
        out[name] = (out[name] * factor).astype(out[name].dtype)
    return out
```

```python
from contextlib import ExitStack
import math

import numpy as np
import concourse.bass as bass
from concourse import mybir

P = 128
D = 1024
KD = D // P
SEQ, CTX = 512, 256
NX, NC = SEQ // P, CTX // P
NT = NX + NC
TOK = SEQ + CTX
HD = 64
SLAB = 512
RING = 3
EPS = 1e-6
GRID_W = 64
ROPE_BASE = 10000.0

A_HEADS, A_KV = 8, 2
A_GROUP = A_HEADS // A_KV
A_W = A_HEADS * HD
A_KVW = A_KV * HD
B_HEADS, B_G, B_N = 16, 2, 128
B_INNER = D
TAPS = 5
XBC = B_INNER + 2 * B_G * B_N
FT = XBC // P
COL_Q, COL_K = 0, A_W
COL_V = COL_K + A_KVW
COL_GA = COL_V + A_KVW
COL_Z = COL_GA + A_W
COL_XBC = COL_Z + B_INNER
COL_DT = COL_XBC + XBC
KVDT = 2 * A_KVW + 2 * B_HEADS
EVEN_MIX = A_W + B_INNER
KM = EVEN_MIX // P
C_HEADS, C_V = 8, 128
LAMBDA_INIT = 0.8 - 0.6 * math.exp(-0.3)
SCALE = HD ** -0.5
NEG = -1e30

F32 = mybir.dt.float32
BF16 = mybir.dt.bfloat16
ALU = mybir.AluOpType
ACT = mybir.ActivationFunctionType
AXX = mybir.AxisListType.X

ROW_C, ROW_CC, ROW_NORM, ROW_MODB = 0, 8, 16, 32
ROWS1 = 64
ROW_TAP, ROW_CONVB, ROW_SSM, ROW_HEAD = 0, TAPS * FT, TAPS * FT + FT, TAPS * FT + FT + KD
ROWS2 = ROW_HEAD + 1

SEGS = (("x", 0, SEQ, NX), ("c", SEQ, CTX, NC))


def stages_layer0():
    st = [("params", 0), ("params", 1)]
    st += [("mod", 0, s) for s in range(4)]
    st += [("modcol", 0)]
    st += [("norm", 0, t) for t in range(NT)]
    st += [("trn", 0, k, s) for k in range(KD) for s in range(2)]
    conv_order = [8, 9, 10, 11, 0, 1, 2, 3, 4, 5, 6, 7]
    for n, f in enumerate(conv_order):
        st.append(("xbc", f, 0))
        if n >= 1:
            st.append(("silu", conv_order[n - 1]))
        st.append(("xbc", f, 1))
        if n >= 1 and conv_order[n - 1] not in (10, 11):
            st.append(("xtr", conv_order[n - 1]))
    st += [("kvdt", 0), ("silu", conv_order[-1]), ("kvdt", 1), ("xtr", conv_order[-1])]
    st += [("kvdt", t) for t in range(2, NT)]
    st += [("dt", 0), ("dt", 1)]
    fill = []
    fill += [("ga", f, s) for f in range(4) for s in range(2)]
    fill += [("mod", 0, 4), ("mod", 0, 5)] + [("mod", 1, s) for s in range(6)]
    steps = [(1, 5), (1, 4), (1, 3), (1, 2), (1, 1), (1, 0), (0, 4), (0, 5), (0, 0), (0, 1), (0, 2), (0, 3)]
    quads = [(d, c, q) for d, c in steps for q in (1, 0, 3, 2)]
    for n in range(len(quads) + 2):
        if n < len(quads):
            d, c, q = quads[n]
            if n % 4 == 0:
                st.append(("cb", d, c))
            st.append(("seg", d, c, q))
        if n >= 2:
            d, c, q = quads[n - 2]
            st.append(("intra", d, c, q))
            if q % 2 == 0:
                st.append(("ysum", d, c, q // 2))
        if n < len(quads) and n % 4 in (1, 2):
            st.append((("inter", "state")[n % 4 - 1],) + quads[n][:2])
        if n % 3 == 1 and fill:
            st.append(fill.pop(0))
    st += fill + [("xres",), ("gates", 0)]
    for t in range(NT):
        st += [("q", t)]
        if t >= 1:
            st += [("qtr", t - 1)]
    st.append(("qtr", NT - 1))
    att = [(t, g) for t in range(NT) for g in range(A_KV)]
    heads = [(t, g, i) for t, g in att for i in range(A_GROUP)]
    fill = [("z", t, n) for n in range(2) for t in range(NT)]
    for n in range(len(heads) + 1):
        if n < len(heads):
            st.append(("score",) + heads[n])
        if n >= 1:
            st.append(("ptr",) + heads[n - 1])
            if heads[n - 1][2] == A_GROUP - 1:
                st.append(("pv",) + heads[n - 1][:2])
        if n % 4 == 1 and fill:
            st.append(fill.pop(0))
    st += fill
    st += [("ynorm", t) for t in range(NT)]
    st += [("ytr", k, s) for k in range(KD) for s in range(2)]
    st += [("out0", n, t) for n in range(2) for t in range(NT)]
    return st


def stages_layer1():
    st = [("modcol", 1)]
    st += [("norm", 1, t) for t in range(NT)]
    st += [("trn", 1, k, s) for k in range(KD) for s in range(2)]
    st += [("k1", n, t) for n in range(2) for t in range(NT)]
    st += [("v1", n, t) for n in range(2) for t in range(NT)]
    st += [("q1", 0, t) for t in range(NX)]
    fill = [("g1", 0, t) for t in range(NX)] + [("q1", 1, t) for t in range(NX)] + [("g1", 1, t) for t in range(NX)]
    work = [(h, t) for h in range(C_HEADS) for t in range(NX)]
    for n in range(len(work) + 2):
        if n < len(work):
            h, t = work[n]
            if t == 0:
                st += [("hq", h), ("hk", h, 0), ("hk", h, 1)]
            st += [("sc1", h, t, 0), ("sc1", h, t, 1)]
        if 1 <= n <= len(work):
            st.append(("ptr1",) + work[n - 1])
        if n >= 2:
            st.append(("pv1",) + work[n - 2])
        if fill:
            st.append(fill.pop(0))
    st += fill + [("gates", 1)]
    st += [("hnorm", t) for t in range(NX)]
    st += [("otr", h) for h in range(C_HEADS)]
    st += [("out1", n, t) for n in range(2) for t in range(NX)]
    return st


STAGES = stages_layer0() + stages_layer1()

def count_stages():
    seen, out = {}, {}
    for s in STAGES:
        seen[s[0]] = seen.get(s[0], 0) + 1
        out[s] = seen[s[0]]
    return out, seen


AT, TOTAL = count_stages()
assert len(AT) == len(STAGES)


def at(*stage):
    return AT[stage]


UNIT_STAGES = ("params", "mod", "modcol", "trn", "xbc", "kvdt", "dt", "q", "ga", "z", "pv", "ytr", "out0",
               "k1", "v1", "q1", "g1", "hq", "hk", "pv1", "otr", "out1")
UNITS = [s for s in STAGES if s[0] in UNIT_STAGES]
UNIT = {s: n for n, s in enumerate(UNITS)}


def slabs_of(stage):
    kind = stage[0]
    if kind == "mod":
        return [stage]
    if kind == "xbc":
        return [("xbc", stage[1] // 4)]
    if kind in ("kvdt", "q", "ga"):
        return [(kind,)]
    if kind == "z":
        return [("z", stage[2])]
    if kind == "out0":
        return [("out0", stage[1], 0), ("out0", stage[1], 1)]
    if kind in ("k1", "v1", "q1", "g1", "out1"):
        return [(kind, stage[1])]
    return []


SLABS, LAST_USE = [], {}
for _s in UNITS:
    for _k in slabs_of(_s):
        if _k not in LAST_USE:
            SLABS.append(_k)
        LAST_USE[_k] = UNIT[_s]
SLAB_NO = {k: n for n, k in enumerate(SLABS)}
SLAB_DMAS = [2 if k == ("kvdt",) else 1 for k in SLABS]


def slab_landed(n):
    return 16 * sum(SLAB_DMAS[m] for m in range(n % RING, n + 1, RING))


def ordinal(kinds):
    return {s: n for n, s in enumerate([s for s in STAGES if s[0] in kinds])}


TR = ordinal(("xtr", "qtr"))
SEGU = ordinal(("cb", "seg"))
FIRST_STEP = ((1, NT - 1), (0, NX))
LAST_STEP = ((1, 0), (0, NX - 1))
STATEU = {}
for _s in STAGES:
    if (_s[0] == "inter" and _s[1:] not in FIRST_STEP) or (_s[0] == "state" and _s[1:] not in LAST_STEP):
        for _g in range(B_G):
            STATEU[_s + (_g,)] = len(STATEU)
STEPS = [s[1:] for s in STAGES if s[0] == "cb"]
STEP = {s: n for n, s in enumerate(STEPS)}
SEG = ordinal(("seg",))
SCORE = ordinal(("score",))
SC1 = ordinal(("sc1",))
HEADU = ordinal(("q", "k1", "q1"))
HEADN = {s: n - NT for s, n in HEADU.items()}
GATE = ordinal(("ga", "z", "g1"))
GATES = list(GATE)
PVS = [s for s in STAGES if s[0] == "pv"]
PV1S = [s for s in STAGES if s[0] == "pv1"]
SEGS_ = list(SEG)


def rope_tables():
    n_freq = HD // 4
    tok = np.arange(SEQ)
    inv = (np.float32(ROPE_BASE) ** (-np.arange(n_freq, dtype=np.float32) / n_freq)).astype(np.float32)
    row = (tok // GRID_W).astype(np.float32)[:, None] * inv
    col = (tok % GRID_W).astype(np.float32)[:, None] * inv
    ang = np.concatenate([row, row, col, col], -1).astype(np.float32)
    cos, sin = np.cos(ang), np.sin(ang)
    sign = np.where((np.arange(HD) // n_freq) % 2 == 0, -1.0, 1.0).astype(np.float32)
    both = np.stack([cos, sin * sign])
    return np.ascontiguousarray(both.reshape(2, NX, P, HD).transpose(2, 0, 1, 3).reshape(P, 2 * NX * HD)
                                ).astype(np.float32)


def triangles():
    k, j = np.arange(P)[:, None], np.arange(P)[None, :]
    parts = [k == j, k <= j, k >= j, k > j, k < j]
    parts = [np.asarray(m, np.float32) for m in parts]
    parts += [np.where(j >= k, 0.0, NEG), np.where(j <= k, 0.0, NEG)]
    return np.ascontiguousarray(np.concatenate(parts, 1)).astype(np.float32)


def build(nc, ins, out):
    x_in, ctx_in = ins["x"].rearrange("a t d -> (a t) d"), ins["ctx"].rearrange("a t d -> (a t) d")
    w_even, w_even_out = ins["ev_w_in"][0], ins["ev_w_out"][0]
    w_odd, w_odd_out = ins["od_w_in"][0], ins["od_w_out"][0]
    out_v = out.rearrange("a t d -> (a t) d")
    mod_dram = nc.dram_tensor("mod_rows_dram", (2, 2, 3 * D), F32, kind="Internal").ap()

    with ExitStack() as ctx:
        def sb(name, width, dt=F32):
            return ctx.enter_context(nc.sbuf_tensor(name, [P, width], dt))[:, :]

        def sem(name):
            return ctx.enter_context(nc.semaphore(name))

        ps = ctx.enter_context(nc.psum_tensor("ps", [P, 8, 512], F32))[:, :, :]

        ring = sb("ring", RING * KD * SLAB)
        hT = sb("hT", KD * TOK).rearrange("p (k t) -> p k t", k=KD)
        xs_all = sb("xs_all", NT * D)
        y_all = sb("y_all", NT * D)
        POOL = 19456
        pool_mem = sb("pool_mem", POOL)

        def carve(start, width):
            assert start + width <= POOL, (start, width)
            return pool_mem[:, start:start + width]

        consts = sb("consts", 5 * P)
        ones = sb("ones", P)
        edges = sb("edges", 3 * P, BF16)
        vec1, vec2 = sb("vec1", ROWS1), sb("vec2", ROWS2)
        halftap = sb("halftap", ROW_SSM)
        silu_c = sb("silu_c", 16)
        mod_cols = sb("mod_cols", 32)
        gain_cols = sb("gain_cols", 16)
        bc = sb("bc", 448)
        qkw = bc[:, 0:256]
        sink, dtb, alog, dskip = bc[:, 256:264], bc[:, 264:296], bc[:, 296:328], bc[:, 328:344]
        nsink, lam = bc[:, 344:352], bc[:, 352:356]
        dtv = sb("dtv", 2 * 192)
        dt_v, dta_v = dtv[:, 0:192], dtv[:, 192:384]
        decay = sb("decay", 384)
        cdec = sb("cdec", 192)
        stat = sb("stat", 192)

        ident, le, ge, gt, lt = (consts[:, n * P:(n + 1) * P] for n in range(5))
        identb, edge_lo, edge_hi = (edges[:, n * P:(n + 1) * P] for n in range(3))

        bct = carve(0, 4 * TOK).rearrange("p (f t) -> p f t", f=4)
        btok = carve(3072, NT * 2 * P).rearrange("p (t g n) -> p t g n", t=NT, g=2)
        gaT = carve(4608, 4 * TOK).rearrange("p (f t) -> p f t", f=4)
        qT = carve(7680, 4 * TOK).rearrange("p (i t) -> p i t", i=4)
        kpad = carve(10752, 2 * TOK).rearrange("p (g t) -> p g t", g=2)
        vdup = carve(12288, NT * 2 * P).rearrange("p (t g u d) -> p t g u d", t=NT, g=2, u=2)
        kraw = carve(13824, NT * P).rearrange("p (t c) -> p t c", t=NT)
        S0 = 14592
        conv = carve(S0, 3 * TOK).rearrange("p (r t) -> p r t", r=3)
        conv_th = carve(S0 + 2304, 2 * TOK).rearrange("p (r t) -> p r t", r=2)
        xsT = carve(7680, 2 * TOK).rearrange("p (r t) -> p r t", r=2)
        dt_tmp = carve(S0, 6 * 192).rearrange("p (r n) -> p r n", r=6)
        dt_raw = carve(9216, 192)
        xdt = carve(7680, 2 * D).rearrange("p (r n) -> p r n", r=2)
        xw = carve(9728, D)
        hst = carve(10752, D)
        cbm = carve(11776, 512).rearrange("p (r g t) -> p r g t", r=2, g=2)
        tri_v = carve(S0, 2 * 512).rearrange("p (r n) -> p r n", r=2)
        emat = carve(S0 + 1024, 3 * 512).rearrange("p (r n) -> p r n", r=3)
        y_in = carve(S0 + 2560, D).rearrange("p (g n) -> p g n", g=2)
        gate_th = carve(S0 + 3584, 512)
        mod_row = carve(S0 + 4096, 512)
        mod_blk = carve(S0 + 4608, P)[0:32, :]
        edges_f32 = carve(2 * P, 2 * P)
        qk = carve(S0, 2 * 640).rearrange("p (r n) -> p r n", r=2)
        qk_sq = carve(S0 + 1280, 640)
        rope_a, rope_b = carve(S0 + 1920, 640), carve(S0 + 2560, 640)
        rope_t = carve(S0 + 3200, 1024).rearrange("p (w a t d) -> p w a t d", w=2, a=2, t=NX)
        rope_raw = carve(3072, 512).rearrange("p (a t d) -> p a t d", a=2, t=NX)
        prob = carve(S0, 2 * 768).rearrange("p (r n) -> p r n", r=2)
        probT = carve(S0 + 1536, 2560).rearrange("p (b i t) -> p b i t", b=5, i=4)
        zg = carve(3072, 512)
        gate_thz = carve(3584, 2 * 512).rearrange("p (r n) -> p r n", r=2)
        prob_junk = carve(S0 + 1536, D)
        gate_bc = carve(0, 2 * D).rearrange("p (s n) -> p s n", s=2)
        gate_b = carve(2048, D)
        res_tmp = carve(S0, 2 * 512).rearrange("p (r n) -> p r n", r=2)
        k1v = carve(0, NT * D).rearrange("p (t n) -> p t n", t=NT)
        q1v = carve(6144, NX * D).rearrange("p (t n) -> p t n", t=NX)
        g1v = carve(10240, NX * D).rearrange("p (t n) -> p t n", t=NX)
        L1 = 14336
        qpad = carve(L1, 2 * SEQ).rearrange("p (c t) -> p c t", c=2)
        kT1 = carve(L1 + 1024, TOK)
        probT1 = carve(L1 + 1792, 768).rearrange("p (b t) -> p b t", b=NT)
        sq1 = carve(L1 + 2560, 512)
        rope_a1, rope_b1 = carve(L1 + 3072, 512), carve(L1 + 3584, 512)
        rope_t1 = carve(L1 + 4096, 1024).rearrange("p (w a t d) -> p w a t d", w=2, a=2, t=NX)
        rope_raw1 = carve(0, 512).rearrange("p (a t d) -> p a t d", a=2, t=NX)
        gate_th1 = xs_all[:, NX * D + 1536:NX * D + 2048]
        prob1 = xs_all[:, NX * D:NX * D + 1536].rearrange("p (c n) -> p c n", c=2)
        gate_bc1, gate_b1 = carve(0, D), carve(D, D)
        res_tmp1 = carve(2 * D, 2 * 512).rearrange("p (r n) -> p r n", r=2)

        xin = xs_all.rearrange("p (t n) -> p t n", t=NT)
        xs = xin
        x1 = xin
        xhat = y_all.rearrange("p (t n) -> p t n", t=NT)
        yacc = xhat
        v1v = xhat
        junk = hT.rearrange("p k t -> p (k t)")[:, 0:D]
        junk1 = carve(7680, D)
        rows1 = carve(0, P)[0:ROWS1, :]
        rows2 = carve(P, P)[0:ROWS2, :]

        ss_x, rs_x = stat[:, 0:12], stat[:, 12:24]
        ss_y, rs_y = stat[:, 24:30], stat[:, 30:36]
        ss_h, rs_h = stat[:, 36:48], stat[:, 48:60]
        ss_o, rs_o = stat[:, 60:92], stat[:, 92:124]
        rmax, rsum, rinv = stat[:, 124:132], stat[:, 132:140], stat[:, 140:148]
        nmax, esink = stat[:, 148:156], stat[:, 156:164]
        neg_half = stat[:, 164:180]
        lam_e = stat[:, 180:184]
        lam_p = dtv[:, 0:256]
        head_gain = stat[:, 184:185]
        neg_lam = stat[:, 185:186]
        lin = ins["od_lambda"]

        slab_in = [sem(f"slab_in{n}") for n in range(RING)]
        unit_ready = sem("unit_ready")
        unit_done = [sem(f"unit_done{n}") for n in range(2)]
        const_in, row_in, bc_in, lam_in, rope_in, rope1_in = (sem(n) for n in (
            "const_in", "row_in", "bc_in", "lam_in", "rope_in", "rope1_in"))
        x_in_s = [sem(f"x_in{t}") for t in range(NT)]
        xres_in, gate_in, gate1_in = sem("xres_in"), sem("gate_in"), sem("gate1_in")
        mod_stored, mod_rows = sem("mod_stored"), sem("mod_rows")
        out_stored = sem("out_stored")
        edges_ready, tanh_c, silu_c_ready, cols_ready = (sem(n) for n in (
            "edges_ready", "tanh_c", "silu_c_ready", "cols_ready"))
        sq_ready, rstd_ready, xhat_ready = sem("sq_ready"), sem("rstd_ready"), sem("xhat_ready")
        conv_tanh, silu_ready, tr_ready, tr_done = (sem(n) for n in (
            "conv_tanh", "silu_ready", "tr_ready", "tr_done"))
        dt_exp, dt_dve, dta_ready = sem("dt_exp"), sem("dt_dve"), sem("dta_ready")
        xdt_ready, xw_ready, tri_ready = sem("xdt_ready"), sem("xw_ready"), sem("tri_ready")
        seg_ready, emat_ready, intra_ready = sem("seg_ready"), sem("emat_ready"), sem("intra_ready")
        seg_done = [sem(f"seg_done{n}") for n in range(2)]
        st_ready, st_done, h_ready, intra_done = (sem(n) for n in ("st_ready", "st_done", "h_ready", "intra_done"))
        gate_tanh, head_sq, head_ss, head_rstd, qk_ready = (sem(n) for n in (
            "gate_tanh", "head_sq", "head_ss", "head_rstd", "qk_ready"))
        score_ready, nmax_ready, prob_ready, probn_ready, pt_ready, pt_done = (sem(n) for n in (
            "score_ready", "nmax_ready", "prob_ready", "probn_ready", "pt_ready", "pt_done"))
        gated_y, y_sq, y_rstd, y_ready, x1_ready = (sem(n) for n in (
            "gated_y", "y_sq", "y_rstd", "y_ready", "x1_ready"))
        gates_ready, pads_ready = sem("gates_ready"), sem("pads_ready")
        o_sq, o_rstd, o_ready, o_gated = sem("o_sq"), sem("o_rstd"), sem("o_ready"), sem("o_gated")
        sc_ready, nmax1, prob1_ready, a_ready, pt1_ready, pt1_done = (sem(n) for n in (
            "sc_ready", "nmax1", "prob1_ready", "a_ready", "pt1_ready", "pt1_done"))
        lam_ready, lam_exp = sem("lam_ready"), sem("lam_exp")
        out_ready = sem("out_ready")
        dve_chain, act_chain, pool_chain = sem("dve_chain"), sem("act_chain"), sem("pool_chain")
        pool_start = sem("pool_start")

        def chained(eng, chain):
            n = [0]

            def link(instr):
                n[0] += 1
                instr.then_inc(chain, 1)
                eng.wait_ge(chain, n[0])
            return link

        def wait_unit(eng, stage):
            eng.wait_ge(unit_ready, UNIT[stage] + 1)

        def wait_done(eng, stage):
            n = UNIT[stage]
            eng.wait_ge(unit_done[n % 2], n // 2 + 1)

        def wait_done_upto(eng, stage):
            n = UNIT[stage]
            for m in (n - 1, n):
                eng.wait_ge(unit_done[m % 2], m // 2 + 1)

        def bank_of(stage):
            return ps[:, UNIT[stage] % 2, :]

        def done_sem(stage):
            return unit_done[UNIT[stage] % 2]

        def pair(n):
            b = 2 + 2 * (n % 2)
            return ps[:, b:b + 2, :].rearrange("p b n -> p (b n)")

        pt_bank = ps[:, 6:8, :].rearrange("p b n -> p (b n)")

        def slab_ap(key):
            n = SLAB_NO[key]
            k = 6 if key[0] == "out0" else KD
            return ring[:, (n % RING) * KD * SLAB:(n % RING) * KD * SLAB + k * SLAB].rearrange(
                "p (k n) -> p k n", k=k)

        def slab_source(key):
            kind = key[0]
            view = lambda w: w.rearrange("(k p) n -> p k n", p=P)
            if kind == "mod":
                return view(ins["mod_w"][key[1]])[:, :, key[2] * SLAB:(key[2] + 1) * SLAB]
            if kind == "xbc":
                return view(w_even)[:, :, COL_XBC + key[1] * SLAB:COL_XBC + (key[1] + 1) * SLAB]
            if kind == "q":
                return view(w_even)[:, :, COL_Q:COL_Q + SLAB]
            if kind == "ga":
                return view(w_even)[:, :, COL_GA:COL_GA + SLAB]
            if kind == "z":
                return view(w_even)[:, :, COL_Z + key[1] * SLAB:COL_Z + (key[1] + 1) * SLAB]
            if kind == "out0":
                return view(w_even_out)[:, 6 * key[2]:6 * key[2] + 6, key[1] * SLAB:(key[1] + 1) * SLAB]
            if kind == "out1":
                return view(w_odd_out)[:, :, key[1] * SLAB:(key[1] + 1) * SLAB]
            first = {"q1": 0, "k1": D, "v1": 2 * D, "g1": 3 * D}[kind] + key[1] * SLAB
            return view(w_odd)[:, :, first:first + SLAB]

        def local_tiles(t):
            return [] if t >= NX else list(range(max(0, t - 1), min(NX - 1, t + 1) + 1))

        block = ctx.enter_context(nc.Block())

        @block.sync
        def _(sp):
            sp.dma_start(consts, ins["tri"][:, 0:5 * P]).then_inc(const_in, 16)
            sp.dma_start(edges_f32, ins["tri"][:, 5 * P:7 * P]).then_inc(const_in, 16)
            r = 0
            for name, count, dst in (("c", 8, rows1), ("c_ctx", 8, rows1), ("norm_w", 16, rows1)):
                src = ins[name]
                src = src.rearrange("a (k p) -> (a k) p", p=P) if len(src.shape) == 2 else \
                    src.rearrange("(k p) -> k p", p=P)
                sp.dma_start(dst[r:r + count, :], src).then_inc(row_in, 16)
                r += count
            for l in range(2):
                sp.dma_start(rows1[ROW_MODB + 16 * l:ROW_MODB + 16 * (l + 1), :],
                             ins["mod_b"][l, 0:2 * D].rearrange("(k p) -> k p", p=P)).then_inc(row_in, 16)
            sp.dma_start(rows2[0:ROW_CONVB, :], ins["ev_conv_w"][0].rearrange("a (k p) -> (a k) p", p=P)
                         ).then_inc(row_in, 16)
            sp.dma_start(rows2[ROW_CONVB:ROW_SSM, :], ins["ev_conv_b"].rearrange("a (k p) -> (a k) p", p=P)
                         ).then_inc(row_in, 16)
            sp.dma_start(rows2[ROW_SSM:ROW_HEAD, :], ins["ev_ssm_norm"].rearrange("a (k p) -> (a k) p", p=P)
                         ).then_inc(row_in, 16)
            sp.dma_start(rows2[ROW_HEAD:ROWS2, :], ins["od_head_norm"]).then_inc(row_in, 16)
            for n, key in enumerate(SLABS):
                if n >= RING:
                    sp.wait_ge(unit_ready, LAST_USE[SLABS[n - RING]] + 1)
                dst, arrived = slab_ap(key), slab_in[n % RING]
                if key == ("kvdt",):
                    view = w_even.rearrange("(k p) n -> p k n", p=P)
                    sp.dma_start(dst[:, :, 0:2 * A_KVW], view[:, :, COL_K:COL_K + 2 * A_KVW]).then_inc(arrived, 16)
                    sp.dma_start(dst[:, :, 2 * A_KVW:KVDT], view[:, :, COL_DT:COL_DT + 2 * B_HEADS]
                                 ).then_inc(arrived, 16)
                else:
                    sp.dma_start(dst, slab_source(key)).then_inc(arrived, 16)
            for n in range(2):
                for t in range(NX):
                    sp.wait_ge(out_ready, at("out1", n, t))
                    sp.dma_start(out_v[t * P:(t + 1) * P, n * SLAB:(n + 1) * SLAB],
                                 x1[:, t, n * SLAB:(n + 1) * SLAB]).then_inc(out_stored, 16)
            sp.wait_ge(out_stored, 16 * 2 * NX)

        @block.tensor
        def _(pe):
            def begin(stage):
                n = UNIT[stage]
                if n >= 2:
                    pe.wait_ge(unit_done[n % 2], n // 2)
                return ps[:, n % 2, :]

            def slabs(stage):
                for key in slabs_of(stage):
                    n = SLAB_NO[key]
                    pe.wait_ge(slab_in[n % RING], slab_landed(n))
                return [slab_ap(key) for key in slabs_of(stage)]

            def project(stage, width, lhs_of, rhs_of, count):
                bank = begin(stage)
                for k in range(count):
                    mm = pe.matmul(bank[:, 0:width], lhs_of(k), rhs_of(k), start=(k == 0), stop=(k == count - 1))
                mm.then_inc(unit_ready, 1)

            def token_major(stage, t, width=SLAB):
                (w,) = slabs(stage)
                project(stage, width, lambda k: hT[:, k, t * P:(t + 1) * P], lambda k: w[:, k, 0:width], KD)

            def feature_major(stage, f, s):
                (w,) = slabs(stage)
                _, first, count, _ = SEGS[s]
                project(stage, count, lambda k: w[:, k, f * P:(f + 1) * P],
                        lambda k: hT[:, k, first:first + count], KD)

            def turn(stage, blocks):
                bank = begin(stage)
                for j, b in enumerate(blocks):
                    mm = pe.transpose(bank[:, j * P:(j + 1) * P], b, ident)
                mm.then_inc(unit_ready, 1)

            for stage in STAGES:
                kind, a = stage[0], stage[1:]
                if kind == "params":
                    rows, count = ((rows1, ROWS1), (rows2, ROWS2))[a[0]]
                    pe.wait_ge(const_in, 32)
                    pe.wait_ge(row_in, 16 * 9)
                    bank = begin(stage)
                    pe.transpose(bank[:, 0:count], rows, ident[0:count, 0:count]).then_inc(unit_ready, 1)
                elif kind == "mod":
                    pe.wait_ge(silu_c_ready, 1)
                    (w,) = slabs(stage)
                    bank = begin(stage)
                    both = silu_c.rearrange("p (r k) -> p k r", r=2)
                    for k in range(KD):
                        mm = pe.matmul(bank[0:2, :], both[:, k, :], w[:, k, :], start=(k == 0), stop=(k == KD - 1))
                    mm.then_inc(unit_ready, 1)
                elif kind == "modcol":
                    pe.wait_ge(mod_rows, 16 * at(*stage))
                    bank = begin(stage)
                    pe.transpose(bank[:, 0:32], mod_blk, ident[0:32, 0:32]).then_inc(unit_ready, 1)
                elif kind == "trn":
                    layer, k, s = a
                    _, first, _, tiles = SEGS[s]
                    pe.wait_ge(xhat_ready, at("norm", layer, first // P + tiles - 1))
                    turn(stage, [xhat[:, first // P + j, k * P:(k + 1) * P] for j in range(tiles)])
                elif kind == "xbc":
                    if stage == ("xbc", 8, 0):
                        wait_done_upto(pe, ("trn", 0, KD - 1, 1))
                    feature_major(stage, a[0] % 4, a[1])
                elif kind in ("xtr", "qtr"):
                    n = TR[stage]
                    if n >= 2:
                        pe.wait_ge(tr_done, n - 1)
                    if kind == "xtr":
                        f = a[0]
                        pe.wait_ge(silu_ready, at("silu", f))
                        src = bct[:, f - 8, :] if f >= 8 else xsT[:, f % 2, :]
                        blocks = [src[:, t * P:(t + 1) * P] for t in range(NT)]
                    else:
                        t = a[0]
                        if t == 0:
                            pe.wait_ge(st_done, len(STATEU))
                            pe.wait_ge(intra_done, 2 * len(STEPS))
                            for b in range(2):
                                pe.wait_ge(seg_done[b], len(SEGU) // 2)
                        pe.wait_ge(qk_ready, t + 1)
                        blocks = [qk[:, t % 2, i * P:(i + 1) * P] for i in range(5)]
                    for j, b in enumerate(blocks):
                        mm = pe.transpose(pair(n)[:, j * P:(j + 1) * P], b, ident)
                    mm.then_inc(tr_ready, 1)
                elif kind == "kvdt":
                    token_major(stage, a[0], KVDT)
                elif kind == "dt":
                    pe.wait_ge(dta_ready, 1)
                    bank = begin(stage)
                    dta = dta_v.rearrange("p (d n) -> p d n", d=2)
                    if a[0] == 0:
                        for j, (m, d) in enumerate(((le, 0), (gt, 0), (ge, 1), (lt, 1))):
                            mm = pe.matmul(bank[:, j * 96:(j + 1) * 96], m, dta[:, d, :], start=(j == 0), stop=True,
                                           skip_group_check=True)
                    else:
                        mm = pe.matmul(bank[:, 0:192], ones, dta_v, start=True, stop=True)
                    mm.then_inc(unit_ready, 1)
                elif kind == "cb":
                    d, c = a
                    n = SEGU[stage]
                    if n == 0:
                        pe.wait_ge(tr_done, sum(1 for s in TR if s[0] == "xtr"))
                    if n >= 2:
                        pe.wait_ge(seg_done[n % 2], n // 2)
                    for g in range(B_G):
                        mm = pe.matmul(ps[:, 2 + n % 2, g * P:(g + 1) * P], bct[:, g, c * P:(c + 1) * P],
                                       bct[:, 2 + g, c * P:(c + 1) * P], start=(g == 0), stop=True,
                                       skip_group_check=True)
                    mm.then_inc(seg_ready, 1)
                elif kind == "seg":
                    d = a[0]
                    n = SEGU[stage]
                    if n >= 2:
                        pe.wait_ge(seg_done[n % 2], n // 2)
                    pe.wait_ge(tri_ready, SEG[stage] + 1)
                    pe.matmul(ps[:, 2 + n % 2, :], (gt, lt)[d], tri_v[:, SEG[stage] % 2, :], start=True, stop=True
                              ).then_inc(seg_ready, 1)
                elif kind in ("inter", "state"):
                    d, c = a
                    if stage + (0,) not in STATEU:
                        continue
                    if kind == "inter":
                        pe.wait_ge(h_ready, STEP[(d, c)] - (d == 0))
                    else:
                        pe.wait_ge(xw_ready, STEP[(d, c)] + 1 - (d == 0))
                    for g in range(B_G):
                        n = STATEU[stage + (g,)]
                        if n >= 2:
                            pe.wait_ge(st_done, n - 1)
                        lhs = bct[:, 2 + g, c * P:(c + 1) * P] if kind == "inter" else btok[:, c, g, :]
                        rhs = (hst if kind == "inter" else xw)[:, g * 512:(g + 1) * 512]
                        pe.matmul(ps[:, (4, 7)[n % 2], :], lhs, rhs, start=True, stop=True).then_inc(st_ready, 1)
                elif kind == "intra":
                    d, c, q = a
                    g, step = q // 2, STEP[(d, c)]
                    if q % 2 == 1 and step > 0:
                        pe.wait_ge(intra_done, 2 * step - 1 + g)
                    pe.wait_ge(emat_ready, SEG[("seg",) + a] + 1)
                    pe.wait_ge(xdt_ready, step + 1)
                    for i in (3, 2, 1, 0):
                        h = 4 * (q % 2) + i
                        left = max(h - 1, 0)
                        mm = pe.matmul(ps[:, 5 + g, left * HD:(h + 1) * HD],
                                       emat[:, SEG[("seg",) + a] % 3, i * P:(i + 1) * P],
                                       xdt[:, step % 2, g * 512 + left * HD:g * 512 + (h + 1) * HD],
                                       start=True, stop=True)
                    mm.then_inc(intra_ready, 1)
                elif kind == "q":
                    token_major(stage, a[0])
                elif kind == "ga":
                    feature_major(stage, a[0], a[1])
                elif kind == "z":
                    token_major(stage, a[0])
                elif kind == "score":
                    t, g, i = a
                    n = SCORE[stage]
                    if n == 0:
                        pe.wait_ge(tr_done, len(TR))
                        pe.wait_ge(edges_ready, 2)
                    if n >= 2:
                        pe.wait_ge(prob_ready, n - 1)
                    lhs, tiles = qT[:, i, t * P:(t + 1) * P], local_tiles(t)
                    bank = pair(n)
                    first = 512 - len(tiles) * P
                    if tiles:
                        pe.matmul(bank[:, first:512], lhs, kpad[:, g, tiles[0] * P:(tiles[-1] + 1) * P],
                                  start=True, stop=True)
                        for j, kt in enumerate(tiles):
                            if kt != t:
                                pe.matmul(bank[:, first + j * P:first + (j + 1) * P], identb,
                                          edge_lo if kt < t else edge_hi, start=False, stop=True,
                                          skip_group_check=True)
                    pe.matmul(bank[:, 512:768], lhs, kpad[:, g, SEQ:TOK], start=True, stop=True
                              ).then_inc(score_ready, 1)
                elif kind == "ptr":
                    t, g, i = a
                    n = SCORE[("score",) + a]
                    if n >= 1:
                        pe.wait_ge(pt_done, n)
                    pe.wait_ge(probn_ready, n + 1)
                    nb = len(local_tiles(t)) + NC
                    for j in range(nb):
                        mm = pe.transpose(pt_bank[:, j * P:(j + 1) * P], prob[:, n % 2, (6 - nb + j) * P:(7 - nb + j) * P],
                                          ident)
                    mm.then_inc(pt_ready, 1)
                elif kind == "pv":
                    t, g = a
                    pe.wait_ge(pt_done, SCORE[("score", t, g, A_GROUP - 1)] + 1)
                    tiles = local_tiles(t) + [NX, NX + 1]
                    bank = begin(stage)
                    for j, kt in enumerate(tiles):
                        mm = pe.matmul(bank, vdup[:, kt, g, :, :], probT[:, j, :, :], start=(j == 0),
                                       stop=(j == len(tiles) - 1))
                    mm.then_inc(unit_ready, 1)
                elif kind == "ytr":
                    k, s = a
                    _, first, _, tiles = SEGS[s]
                    pe.wait_ge(y_ready, at("ynorm", first // P + tiles - 1))
                    turn(stage, [yacc[:, first // P + j, k * P:(k + 1) * P] for j in range(tiles)])
                elif kind == "out0":
                    n, t = a
                    if a == (0, 0):
                        wait_done_upto(pe, ("ytr", KD - 1, 1))
                    w = slabs(stage)
                    project(stage, SLAB,
                            lambda k: (gaT[:, k, :] if k < 4 else hT[:, k - 4, :])[:, t * P:(t + 1) * P],
                            lambda k: w[k // 6][:, k % 6, :], KM)
                elif kind in ("k1", "v1", "q1", "g1"):
                    if stage == ("k1", 0, 0):
                        wait_done_upto(pe, ("trn", 1, KD - 1, 1))
                    token_major(stage, a[1])
                elif kind == "hq":
                    h = a[0]
                    pe.wait_ge(qk_ready, NT + HEADN[("q1", h // 4, NX - 1)] + 1)
                    turn(stage, [q1v[:, t, h * P:(h + 1) * P] for t in range(NX)])
                elif kind == "hk":
                    h, s = a
                    pe.wait_ge(qk_ready, NT + HEADN[("k1", 1, NT - 1)] + 1)
                    turn(stage, [k1v[:, t, h * P:(h + 1) * P] for t in (range(NX) if s == 0 else range(NX, NT))])
                elif kind == "sc1":
                    h, t, c = a
                    n = SC1[stage]
                    if n == 0:
                        pe.wait_ge(prob_ready, len(SCORE))
                    if n >= 2:
                        pe.wait_ge(prob1_ready, n - 1)
                    if (t, c) == (0, 0):
                        wait_done(pe, ("hq", h))
                        wait_done(pe, ("hk", h, 0))
                        wait_done(pe, ("hk", h, 1))
                    for lo, hi in ((0, 512), (512, TOK)):
                        mm = pe.matmul(pair(n)[:, lo:hi], qpad[:, c, t * P:(t + 1) * P], kT1[:, lo:hi],
                                       start=True, stop=True)
                    mm.then_inc(sc_ready, 1)
                elif kind == "ptr1":
                    n = at(*stage) - 1
                    if n == 0:
                        pe.wait_ge(pt_done, len(SCORE))
                    else:
                        pe.wait_ge(pt1_done, n)
                    pe.wait_ge(a_ready, n + 1)
                    for j in range(NT):
                        mm = pe.transpose(pt_bank[:, j * P:(j + 1) * P], prob1[:, 0, j * P:(j + 1) * P], ident)
                    mm.then_inc(pt1_ready, 1)
                elif kind == "pv1":
                    h, t = a
                    pe.wait_ge(pt1_done, at(*stage))
                    if stage == ("pv1", 0, 0):
                        wait_done_upto(pe, ("v1", 1, NT - 1))
                    bank = begin(stage)
                    for j in range(NT):
                        mm = pe.matmul(bank[:, 0:P], probT1[:, j, :], v1v[:, j, h * P:(h + 1) * P],
                                       start=(j == 0), stop=(j == NT - 1))
                    mm.then_inc(unit_ready, 1)
                elif kind == "otr":
                    pe.wait_ge(o_ready, NX)
                    turn(stage, [g1v[:, t, a[0] * P:(a[0] + 1) * P] for t in range(NX)])
                elif kind == "out1":
                    if a == (0, 0):
                        wait_done_upto(pe, ("otr", C_HEADS - 1))
                    token_major(stage, a[1])

        @block.vector
        def _(dve):
            link = chained(dve, dve_chain)
            V = nc.vector

            def ropes(src, groups, wtab, wrow, token_tile, ta, tb):
                v = src.rearrange("p (h d) -> p h d", d=HD)
                a = ta[:, 0:groups * HD].rearrange("p (h d) -> p h d", d=HD)
                if token_tile >= NX:
                    link(V.tensor_tensor(a, v, wrow.unsqueeze(1).to_broadcast([P, groups, HD]), ALU.mult))
                    return
                cos = wtab[:, 0, token_tile, :].unsqueeze(1).to_broadcast([P, groups, HD])
                V.tensor_tensor(a, v, cos, ALU.mult)
                pairs = src.rearrange("p (m b j) -> p m b j", b=2, j=HD // 4)
                turned = tb[:, 0:groups * HD].rearrange("p (m b j) -> p m b j", b=2, j=HD // 4)
                sin = wtab[:, 1, token_tile, :].rearrange("p (a b j) -> p a b j", b=2, j=HD // 4)
                for b in range(2):
                    for half in range(2):
                        o = turned.rearrange("p (h a) b j -> p h a b j", a=2)[:, :, half, b, :]
                        i = pairs.rearrange("p (h a) b j -> p h a b j", a=2)[:, :, half, 1 - b, :]
                        w = sin[:, half, b, :].unsqueeze(1).to_broadcast([P, groups, HD // 4])
                        last = V.tensor_tensor(o, i, w, ALU.mult)
                link(last)
                link(V.tensor_tensor(ta[:, 0:groups * HD], ta[:, 0:groups * HD], tb[:, 0:groups * HD], ALU.add))

            def gain_tables(tab, raw, wq, wk):
                for w, row in ((0, wq), (1, wk)):
                    V.tensor_tensor(tab[:, w, 0, :, :], raw[:, 0, :, :],
                                    row.unsqueeze(1).to_broadcast([P, NX, HD]), ALU.mult)
                    m = row.rearrange("p (a b j) -> p a b j", a=2, b=2)
                    for half in range(2):
                        for b in range(2):
                            at_ = slice((2 * half + b) * 16, (2 * half + b + 1) * 16)
                            last = V.tensor_tensor(tab[:, w, 1, :, at_], raw[:, 1, :, at_],
                                                   m[:, half, 1 - b, :].unsqueeze(1).to_broadcast([P, NX, 16]),
                                                   ALU.mult)
                link(last)

            V.memset(ones, 1.0)
            V.memset(neg_half, -0.5).then_inc(pool_start, 1)
            dve.wait_ge(const_in, 32)
            V.tensor_copy(identb, ident).then_inc(edges_ready, 1)
            V.tensor_copy(edges[:, P:3 * P], edges_f32).then_inc(edges_ready, 1)

            for stage in STAGES:
                kind, a = stage[0], stage[1:]
                if kind == "params":
                    wait_unit(dve, stage)
                    dst, count = ((vec1, ROWS1), (vec2, ROWS2))[a[0]]
                    V.tensor_copy(dst, bank_of(stage)[:, 0:count]).then_inc(done_sem(stage), 1)
                    wait_done(dve, stage)
                    if a[0] == 0:
                        dve.wait_ge(tanh_c, 1)
                        link(V.scalar_tensor_tensor(out=silu_c, in0=silu_c, scalar=1.0, in1=vec1[:, 0:16],
                                                    op0=ALU.add, op1=ALU.mult))
                        V.tensor_scalar(silu_c, silu_c, 0.5, None, ALU.mult).then_inc(silu_c_ready, 1)
                    else:
                        link(V.tensor_scalar(halftap, vec2[:, 0:ROW_SSM], 0.5, None, ALU.mult))
                        link(V.tensor_scalar(head_gain, vec2[:, ROW_HEAD:ROW_HEAD + 1],
                                             0.5 * (1.0 - LAMBDA_INIT), None, ALU.mult))
                        dve.wait_ge(bc_in, 16 * 8)
                        link(V.tensor_scalar(nsink, sink, -1.0, None, ALU.mult))
                elif kind == "modcol":
                    layer = a[0]
                    wait_unit(dve, stage)
                    cols = mod_cols.rearrange("p (r n) -> p r n", r=2)
                    V.tensor_tensor(cols, bank_of(stage)[:, 0:32].rearrange("p (r n) -> p r n", r=2),
                                    vec1[:, ROW_MODB + 16 * layer:ROW_MODB + 16 * (layer + 1)].unsqueeze(1)
                                    .to_broadcast([P, 2, 16]), ALU.add).then_inc(done_sem(stage), 1)
                    wait_done(dve, stage)
                    gains = gain_cols.rearrange("p (r n) -> p r n", r=2)
                    V.scalar_tensor_tensor(
                        out=gains, in0=cols[:, :, 8:16], scalar=1.0,
                        in1=vec1[:, ROW_NORM + 8 * layer:ROW_NORM + 8 * (layer + 1)].unsqueeze(1)
                        .to_broadcast([P, 2, 8]), op0=ALU.add, op1=ALU.mult).then_inc(cols_ready, 1)
                elif kind == "norm":
                    layer, t = a
                    dve.wait_ge(rstd_ready, at(*stage))
                    V.tensor_scalar(xhat[:, t, :], xin[:, t, :], rs_x[:, layer * NT + t:layer * NT + t + 1], None,
                                    ALU.mult).then_inc(xhat_ready, 1)
                elif kind == "trn":
                    layer, k, s = a
                    if s == 0:
                        dve.wait_ge(cols_ready, at("modcol", layer))
                        wait_unit(dve, stage)
                        V.tensor_scalar(hT[:, k, 0:SEQ], bank_of(stage), gain_cols[:, k:k + 1], mod_cols[:, k:k + 1],
                                        ALU.mult, ALU.add).then_inc(done_sem(stage), 1)
                elif kind == "xbc":
                    f, s = a
                    _, first, count, _ = SEGS[s]
                    wait_unit(dve, stage)
                    src = bank_of(stage)
                    dst = conv[:, (at("xbc", f, 0) // 2) % 3, first:first + count]
                    tap = lambda j: halftap[:, j * FT + f:j * FT + f + 1]
                    link(V.tensor_scalar(dst, src[:, 0:count], tap(2), halftap[:, ROW_CONVB + f:ROW_CONVB + f + 1],
                                         ALU.mult, ALU.add))
                    for j in (0, 1, 3, 4):
                        lo, hi = max(0, 2 - j), min(count, count + 2 - j)
                        ins_ = V.scalar_tensor_tensor(out=dst[:, lo:hi], in0=src[:, lo + j - 2:hi + j - 2],
                                                      scalar=tap(j), in1=dst[:, lo:hi], op0=ALU.mult, op1=ALU.add)
                        if j < 4:
                            link(ins_)
                        else:
                            ins_.then_inc(done_sem(stage), 1)
                elif kind == "silu":
                    f = a[0]
                    n = at(*stage) - 1
                    dve.wait_ge(conv_tanh, n + 1)
                    wait_done_upto(dve, ("xbc", f, 1))
                    src = conv[:, (at("xbc", f, 0) // 2) % 3, :]
                    if f >= 8:
                        dst = bct[:, f - 8, :]
                    else:
                        dst = xsT[:, f % 2, :]
                        if f >= 2:
                            dve.wait_ge(tr_ready, TR[("xtr", f - 2)] + 1)
                    V.scalar_tensor_tensor(out=dst, in0=conv_th[:, n % 2, :], scalar=1.0, in1=src,
                                           op0=ALU.add, op1=ALU.mult).then_inc(silu_ready, 1)
                elif kind == "dt":
                    if a[0] == 0:
                        wait_done_upto(dve, ("kvdt", NT - 1))
                        raw4 = dt_raw.rearrange("p (t d h) -> p d t h", t=NT, d=2)
                        v, e, u, w, m, n_ = (dt_tmp[:, j, :] for j in range(6))
                        v4 = v.rearrange("p (d t h) -> p d t h", d=2, t=NT)
                        for d in range(2):
                            last = V.tensor_tensor(v4[:, d, :, :], raw4[:, d, :, :],
                                                   dtb[:, d * 16:(d + 1) * 16].unsqueeze(1)
                                                   .to_broadcast([P, NT, 16]), ALU.add)
                        link(last)
                        link(V.tensor_scalar(m, v, -1.0, None, ALU.mult))
                        V.tensor_tensor(n_, v, m, ALU.min).then_inc(dt_dve, 1)
                        dve.wait_ge(dt_exp, 1)
                        link(V.tensor_scalar(u, e, 1.0, None, ALU.add))
                        link(V.tensor_scalar(w, u, 1.0, 2.0 ** -24, ALU.subtract, ALU.max))
                        V.tensor_scalar(m, u, 0.0, None, ALU.add).then_inc(dt_dve, 1)
                        link(V.reciprocal(w, w))
                        link(V.tensor_tensor(w, w, e, ALU.mult))
                        dve.wait_ge(dt_exp, 2)
                        link(V.tensor_tensor(w, w, m, ALU.mult))
                        link(V.scalar_tensor_tensor(out=dt_v, in0=v, scalar=0.0, in1=w, op0=ALU.max, op1=ALU.add))
                        dve.wait_ge(dt_exp, 3)
                        link(V.tensor_scalar(alog, alog, -1.0, None, ALU.mult))
                        for d in range(2):
                            last = V.tensor_tensor(
                                dta_v[:, d * 96:(d + 1) * 96].rearrange("p (t h) -> p t h", t=NT),
                                dt_v[:, d * 96:(d + 1) * 96].rearrange("p (t h) -> p t h", t=NT),
                                alog[:, d * 16:(d + 1) * 16].unsqueeze(1).to_broadcast([P, NT, 16]), ALU.mult)
                            if d == 0:
                                link(last)
                        last.then_inc(dta_ready, 1)
                elif kind == "cb":
                    d, c = a
                    n = SEGU[stage]
                    dve.wait_ge(seg_ready, n + 1)
                    r = STEP[a] % 2
                    V.tensor_tensor(cbm[:, r, :, :], ps[:, 2 + n % 2, 0:2 * P].rearrange("p (g t) -> p g t", g=2),
                                    (le, ge)[d].unsqueeze(1).to_broadcast([P, 2, P]), ALU.mult
                                    ).then_inc(seg_done[n % 2], 1)
                    dve.wait_ge(seg_done[n % 2], n // 2 + 1)
                elif kind == "seg":
                    d, c, q = a
                    n, u = SEG[stage], SEGU[stage]
                    dve.wait_ge(seg_done[u % 2], u // 2 + 1)
                    e = emat[:, n % 3, :].rearrange("p (h t) -> p h t", h=4)
                    V.tensor_tensor(e, e, cbm[:, STEP[(d, c)] % 2, q // 2, :].unsqueeze(1).to_broadcast([P, 4, P]),
                                    ALU.mult).then_inc(emat_ready, 1)
                elif kind == "inter":
                    d, c = a
                    if stage + (0,) in STATEU:
                        for g in range(B_G):
                            n = STATEU[stage + (g,)]
                            dve.wait_ge(st_ready, n + 1)
                            ela = decay[:, 2 * d * 96 + c * 16 + g * 8:2 * d * 96 + c * 16 + g * 8 + 8]
                            V.tensor_tensor(y_in[:, g, :].rearrange("p (h d) -> p h d", h=8),
                                            ps[:, (4, 7)[n % 2], :].rearrange("p (h d) -> p h d", h=8),
                                            ela.unsqueeze(2).to_broadcast([P, 8, HD]), ALU.mult).then_inc(st_done, 1)
                        dve.wait_ge(st_done, n + 1)
                elif kind == "state":
                    d, c = a
                    if stage + (0,) in STATEU:
                        first = a in FIRST_STEP
                        if not first:
                            cd = cdec[:, d * 96 + c * 16:d * 96 + c * 16 + 16]
                            h3 = hst.rearrange("p (h d) -> p h d", h=16)
                            link(V.tensor_tensor(h3, h3, cd.unsqueeze(2).to_broadcast([P, 16, HD]), ALU.mult))
                        for g in range(B_G):
                            n = STATEU[stage + (g,)]
                            dve.wait_ge(st_ready, n + 1)
                            part, src = hst[:, g * 512:(g + 1) * 512], ps[:, (4, 7)[n % 2], :]
                            if first:
                                V.tensor_copy(part, src).then_inc(st_done, 1)
                            else:
                                V.tensor_tensor(part, part, src, ALU.add).then_inc(st_done, 1)
                        dve.wait_ge(st_done, n + 1)
                        V.tensor_copy(stat[:, 186:187], ones[:, 0:1]).then_inc(h_ready, 1)
                elif kind == "ysum":
                    d, c, g = a
                    step = STEP[(d, c)]
                    dve.wait_ge(intra_ready, SEG[("seg", d, c, 2 * g)] + 1)
                    part = yacc[:, c, g * 512:(g + 1) * 512]
                    if (d, c) in FIRST_STEP:
                        dve.wait_ge(xdt_ready, step + 1)
                        V.tensor_tensor(part, part, ps[:, 5 + g, :], ALU.add).then_inc(intra_done, 1)
                    else:
                        V.tensor_tensor(y_in[:, g, :], y_in[:, g, :], ps[:, 5 + g, :], ALU.add
                                        ).then_inc(intra_done, 1)
                        dve.wait_ge(intra_done, 2 * step + g + 1)
                        dve.wait_ge(xdt_ready, step + 1)
                        link(V.tensor_tensor(part, part, y_in[:, g, :], ALU.add))
                elif kind == "ga":
                    f, s = a
                    _, first, count, _ = SEGS[s]
                    n = GATE[stage]
                    dve.wait_ge(gate_tanh, n + 1)
                    V.scalar_tensor_tensor(out=gaT[:, f, first:first + count], in0=gate_th[:, 0:count],
                                           scalar=1.0, in1=bank_of(stage)[:, 0:count], op0=ALU.add, op1=ALU.mult
                                           ).then_inc(done_sem(stage), 1)
                elif kind in ("q", "k1", "q1"):
                    n = HEADU[stage]
                    groups = 10 if kind == "q" else 8
                    t = a[-1]
                    if n == 0:
                        dve.wait_ge(rope_in, 16)
                        gain_tables(rope_t, rope_raw, qkw[:, 0:64], qkw[:, 64:128])
                        V.memset(kpad[HD:P, 0, :], 0.0)
                        V.memset(kpad[0:HD, 1, :], 0.0).then_inc(pads_ready, 1)
                    if stage == ("k1", 0, 0):
                        dve.wait_ge(rope1_in, 16)
                        dve.wait_ge(x1_ready, 2 * NT)
                        gain_tables(rope_t1, rope_raw1, qkw[:, 128:192], qkw[:, 192:256])
                        V.memset(qpad[HD:P, 0, :], 0.0)
                        V.memset(qpad[0:HD, 1, :], 0.0).then_inc(pads_ready, 1)
                        dve.wait_ge(lam_in, 16)
                        l4 = lam_p.rearrange("p (a b d) -> p a b d", a=2, b=2)
                        link(V.tensor_tensor(l4[:, :, 0, :], l4[:, :, 0, :], l4[:, :, 1, :], ALU.mult))
                        V.tensor_reduce(lam_e[:, 0:2], l4[:, :, 0, :], AXX, ALU.add).then_inc(lam_ready, 1)
                    sq = (qk_sq if kind == "q" else sq1)[:, 0:groups * HD]
                    if n >= 1:
                        dve.wait_ge(qk_ready, n)
                    dve.wait_ge(head_sq, n + 1)
                    V.tensor_reduce(ss_h[:, 0:groups], sq.rearrange("p (h d) -> p h d", d=HD), AXX, ALU.add
                                    ).then_inc(head_ss, 1)
                    if kind == "q":
                        buf, ta = qk[:, t % 2, :], rope_a
                        ropes(buf[:, 0:A_W], 8, rope_t[:, 0], qkw[:, 0:64], t, rope_a, rope_b)
                        ropes(buf[:, A_W:640], 2, rope_t[:, 1], qkw[:, 64:128], t, rope_a[:, A_W:640],
                              rope_b[:, A_W:640])
                    else:
                        buf = (k1v if kind == "k1" else q1v)[:, t, a[0] * SLAB:(a[0] + 1) * SLAB]
                        w = 1 if kind == "k1" else 0
                        ta = rope_a1
                        ropes(buf, 8, rope_t1[:, w], qkw[:, 128 + 64 * w:192 + 64 * w], t, rope_a1, rope_b1)
                    dve.wait_ge(head_rstd, n + 1)
                    if kind == "q":
                        for g in range(A_KV):
                            V.tensor_tensor(
                                buf[:, 0:A_W].rearrange("p (i g d) -> p g i d", g=A_KV, d=HD)[:, g, :, :],
                                ta[:, g * 256:(g + 1) * 256].rearrange("p (i d) -> p i d", d=HD),
                                rs_h[:, 4 * g:4 * g + 4].unsqueeze(2).to_broadcast([P, A_GROUP, HD]), ALU.mult)
                        buf, ta, first, groups = buf[:, A_W:640], ta[:, A_W:640], 8, 2
                    else:
                        first = 0
                    V.tensor_tensor(buf.rearrange("p (h d) -> p h d", d=HD),
                                    ta[:, 0:groups * HD].rearrange("p (h d) -> p h d", d=HD),
                                    rs_h[:, first:first + groups].unsqueeze(2).to_broadcast([P, groups, HD]), ALU.mult
                                    ).then_inc(qk_ready, 1)
                elif kind in ("score", "sc1"):
                    if kind == "score":
                        t, g, i = a
                        n = SCORE[stage]
                        dve.wait_ge(score_ready, n + 1)
                        first = 512 - len(local_tiles(t)) * P
                        r = n % 8
                        link(V.tensor_reduce(rmax[:, r:r + 1], pair(n)[:, first:768], AXX, ALU.max))
                        h = 4 * g + i
                        V.tensor_scalar(nmax[:, r:r + 1], rmax[:, r:r + 1], -SCALE, nsink[:, h:h + 1],
                                        ALU.mult, ALU.min).then_inc(nmax_ready, 1)
                    else:
                        n = SC1[stage]
                        dve.wait_ge(sc_ready, n + 1)
                        r = n % 8
                        link(V.tensor_reduce(rmax[:, r:r + 1], pair(n)[:, 0:TOK], AXX, ALU.max))
                        V.tensor_scalar(nmax[:, r:r + 1], rmax[:, r:r + 1], -SCALE, None, ALU.mult
                                        ).then_inc(nmax1, 1)
                elif kind == "ptr":
                    t, g, i = a
                    n = SCORE[("score",) + a]
                    r, first = n % 8, 512 - len(local_tiles(t)) * P
                    dve.wait_ge(prob_ready, n + 1)
                    link(V.tensor_scalar(rinv[:, r:r + 1], rsum[:, r:r + 1], esink[:, r:r + 1], 2.0, ALU.add, ALU.mult))
                    link(V.reciprocal(rinv[:, r:r + 1], rinv[:, r:r + 1]))
                    V.tensor_scalar(prob[:, n % 2, first:768], prob[:, n % 2, first:768], rinv[:, r:r + 1], None,
                                    ALU.mult).then_inc(probn_ready, 1)
                elif kind == "pv":
                    t, g = a
                    wait_unit(dve, stage)
                    src = bank_of(stage).rearrange("p (j u t) -> p u j t", u=2, t=P)
                    for half in range(2):
                        rows = slice(half * HD, (half + 1) * HD)
                        dst = gaT[rows, 2 * g:2 * g + 2, t * P:(t + 1) * P]
                        last = V.tensor_tensor(dst, src[rows, half, :, :], dst, ALU.mult)
                    last.then_inc(done_sem(stage), 1)
                elif kind == "z":
                    t, n_ = a
                    n = GATE[stage]
                    dve.wait_ge(gate_tanh, n + 1)
                    V.scalar_tensor_tensor(out=zg, in0=gate_thz[:, n % 2, :], scalar=1.0, in1=bank_of(stage),
                                           op0=ALU.add, op1=ALU.mult).then_inc(done_sem(stage), 1)
                    wait_done(dve, stage)
                    part = yacc[:, t, n_ * SLAB:(n_ + 1) * SLAB]
                    V.tensor_tensor(part, part, zg, ALU.mult).then_inc(gated_y, 1)
                elif kind == "ynorm":
                    t = a[0]
                    dve.wait_ge(y_rstd, t + 1)
                    V.tensor_scalar(yacc[:, t, :], yacc[:, t, :], rs_y[:, t:t + 1], 0.5, ALU.mult, ALU.mult
                                    ).then_inc(y_ready, 1)
                elif kind == "ytr":
                    k, s = a
                    if s == 0:
                        wait_unit(dve, stage)
                        V.tensor_scalar(hT[:, k, 0:SEQ], bank_of(stage), vec2[:, ROW_SSM + k:ROW_SSM + k + 1], None,
                                        ALU.mult).then_inc(done_sem(stage), 1)
                elif kind == "gates":
                    layer = a[0]
                    if layer == 0:
                        dve.wait_ge(gate_in, 16 * 3)
                        link(V.tensor_tensor(gate_bc, gate_bc, gate_b.unsqueeze(1).to_broadcast([P, 2, D]), ALU.add))
                    else:
                        dve.wait_ge(gate1_in, 16 * 2)
                        link(V.tensor_tensor(gate_bc1, gate_bc1, gate_b1, ALU.add))
                elif kind in ("out0", "out1"):
                    n, t = a
                    u = at(*stage) - 1
                    if stage == ("out0", 0, 0):
                        dve.wait_ge(xres_in, 16 * NT)
                    wait_unit(dve, stage)
                    if kind == "out0":
                        tmp, gate = res_tmp[:, u % 2, :], gate_bc[:, 0 if t < NX else 1, n * SLAB:(n + 1) * SLAB]
                    else:
                        tmp, gate = res_tmp1[:, u % 2, :], gate_bc1[:, n * SLAB:(n + 1) * SLAB]
                    if u >= 2:
                        dve.wait_ge(x1_ready if kind == "out0" else out_ready, u - 1)
                    V.tensor_tensor(tmp, bank_of(stage), gate, ALU.mult).then_inc(done_sem(stage), 1)
                    wait_done(dve, stage)
                    part = x1[:, t, n * SLAB:(n + 1) * SLAB]
                    V.tensor_tensor(part, part, tmp, ALU.add).then_inc(x1_ready if kind == "out0" else out_ready, 1)
                elif kind == "g1":
                    n_, t = a
                    n = GATE[stage]
                    dve.wait_ge(gate_tanh, n + 1)
                    V.scalar_tensor_tensor(out=g1v[:, t, n_ * SLAB:(n_ + 1) * SLAB], in0=gate_th1, scalar=1.0,
                                           in1=bank_of(stage), op0=ALU.add, op1=ALU.mult
                                           ).then_inc(done_sem(stage), 1)
                elif kind == "ptr1":
                    h, t = a
                    n = at(*stage) - 1
                    if n == 0:
                        dve.wait_ge(lam_exp, 1)
                        link(V.tensor_tensor(neg_lam, lam_e[:, 3:4], lam_e[:, 2:3], ALU.subtract))
                        link(V.tensor_scalar(neg_lam, neg_lam, -LAMBDA_INIT, None, ALU.add))
                    dve.wait_ge(prob1_ready, 2 * n + 2)
                    r = (2 * n) % 8
                    link(V.reciprocal(rinv[:, r:r + 2], rsum[:, r:r + 2]))
                    link(V.tensor_tensor(rinv[:, r + 1:r + 2], rinv[:, r + 1:r + 2], neg_lam, ALU.mult))
                    link(V.tensor_scalar(prob1[:, 1, :], prob1[:, 1, :], rinv[:, r + 1:r + 2], None, ALU.mult))
                    V.scalar_tensor_tensor(out=prob1[:, 0, :], in0=prob1[:, 0, :], scalar=rinv[:, r:r + 1],
                                           in1=prob1[:, 1, :], op0=ALU.mult, op1=ALU.add).then_inc(a_ready, 1)
                elif kind == "pv1":
                    h, t = a
                    dve.wait_ge(o_sq, at(*stage))
                    if h % 4 == 0:
                        wait_done(dve, ("g1", h // 4, t))
                    part = g1v[:, t, h * P:(h + 1) * P]
                    V.tensor_tensor(part, bank_of(stage)[:, 0:P], part, ALU.mult).then_inc(done_sem(stage), 1)
                elif kind == "hnorm":
                    t = a[0]
                    dve.wait_ge(o_rstd, t + 1)
                    wait_done_upto(dve, ("pv1", C_HEADS - 1, NX - 1))
                    g3 = g1v[:, t, :].rearrange("p (h d) -> p h d", h=C_HEADS)
                    V.tensor_tensor(g3, g3, rs_o[:, t * 8:(t + 1) * 8].unsqueeze(2).to_broadcast([P, C_HEADS, P]),
                                    ALU.mult).then_inc(o_ready, 1)
                elif kind == "otr":
                    h = a[0]
                    if h % 2 == 0:
                        wait_unit(dve, stage)
                        V.tensor_scalar(hT[:, h, 0:SEQ], bank_of(stage), head_gain, None, ALU.mult
                                        ).then_inc(done_sem(stage), 1)

        @block.scalar
        def _(act):
            link = chained(act, act_chain)
            A = nc.scalar
            for stage in STAGES:
                kind, a = stage[0], stage[1:]
                if kind == "params" and a[0] == 0:
                    wait_done(act, stage)
                    A.activation(silu_c, vec1[:, 0:16], ACT.Tanh, scale=0.5).then_inc(tanh_c, 1)
                elif kind == "mod":
                    layer, s = a
                    m = at(*stage) - 1
                    wait_unit(act, stage)
                    if m >= 1:
                        act.wait_ge(mod_stored, 16 * m)
                    A.copy(mod_row[0:2, :], bank_of(stage)[0:2, :]).then_inc(done_sem(stage), 1)
                    wait_done(act, stage)
                    act.dma_start(mod_dram[layer, :, s * SLAB:(s + 1) * SLAB], mod_row[0:2, :]
                                  ).then_inc(mod_stored, 16)
                elif kind == "modcol":
                    layer = a[0]
                    act.wait_ge(mod_stored, 16 * at("mod", layer, 3 if layer == 0 else 5))
                    act.dma_start(mod_blk, mod_dram[layer, :, 0:2 * D].rearrange("r (k p) -> r k p", p=P)
                                  ).then_inc(mod_rows, 16)
                elif kind == "norm":
                    layer, t = a
                    if layer == 0:
                        act.wait_ge(x_in_s[t], 16)
                    else:
                        act.wait_ge(x1_ready, at("out0", 1, t))
                    if at(*stage) > 1:
                        act.wait_ge(sq_ready, at(*stage) - 1)
                    A.activation(junk if layer == 0 else junk1, xin[:, t, :], ACT.Square, accum_out=ss_x[:, layer * NT + t:layer * NT + t + 1]
                                 ).then_inc(sq_ready, 1)
                elif kind == "trn":
                    layer, k, s = a
                    if s == 1:
                        act.wait_ge(cols_ready, at("modcol", layer))
                        wait_unit(act, stage)
                        A.activation(hT[:, k, SEQ:TOK], bank_of(stage)[:, 0:CTX], ACT.Identity,
                                     scale=gain_cols[:, 8 + k:9 + k], bias=mod_cols[:, 16 + k:17 + k]
                                     ).then_inc(done_sem(stage), 1)
                elif kind == "silu":
                    f = a[0]
                    n = at(*stage) - 1
                    wait_done_upto(act, ("xbc", f, 1))
                    if n >= 2:
                        act.wait_ge(silu_ready, n - 1)
                    A.activation(conv_th[:, n % 2, :], conv[:, (at("xbc", f, 0) // 2) % 3, :], ACT.Tanh
                                 ).then_inc(conv_tanh, 1)
                elif kind == "xtr":
                    f = a[0]
                    act.wait_ge(tr_ready, TR[stage] + 1)
                    src = pair(TR[stage])[:, 0:TOK].rearrange("p (t n) -> p t n", t=NT)
                    dst = btok[:, :, f - 8, :] if f >= 8 else xs[:, :, f * P:(f + 1) * P]
                    A.copy(dst, src).then_inc(tr_done, 1)
                elif kind == "kvdt":
                    t = a[0]
                    wait_unit(act, stage)
                    bank = bank_of(stage)
                    A.copy(kraw[:, t, :], bank[:, 0:P])
                    A.copy(vdup[:, t, :, :, :], bank[:, P:2 * P].rearrange("p (g d) -> p g d", g=2).unsqueeze(2)
                           .to_broadcast([P, 2, 2, HD]))
                    A.copy(dt_raw[:, t * 32:(t + 1) * 32], bank[:, 2 * P:KVDT]).then_inc(done_sem(stage), 1)
                elif kind == "dt":
                    if a[0] == 0:
                        v, e, u, w, m, n_ = (dt_tmp[:, j, :] for j in range(6))
                        act.wait_ge(dt_dve, 1)
                        A.activation(e, n_, ACT.Exp).then_inc(dt_exp, 1)
                        act.wait_ge(dt_dve, 2)
                        A.activation(m, m, ACT.Ln).then_inc(dt_exp, 1)
                        A.activation(alog, alog, ACT.Exp).then_inc(dt_exp, 1)
                        wait_unit(act, stage)
                        A.activation(decay, bank_of(stage)[:, 0:384], ACT.Exp).then_inc(done_sem(stage), 1)
                    else:
                        wait_unit(act, stage)
                        A.activation(cdec, bank_of(stage)[:, 0:192], ACT.Exp).then_inc(done_sem(stage), 1)
                elif kind == "seg":
                    n, u = SEG[stage], SEGU[stage]
                    act.wait_ge(seg_ready, u + 1)
                    if n >= 3:
                        act.wait_ge(intra_ready, n - 2)
                    A.activation(emat[:, n % 3, :], ps[:, 2 + u % 2, :], ACT.Exp).then_inc(seg_done[u % 2], 1)
                elif kind in ("ga", "z", "g1"):
                    n = GATE[stage]
                    count = SEGS[a[1]][2] if kind == "ga" else SLAB
                    wait_unit(act, stage)
                    dst = {"ga": gate_th[:, 0:count], "z": gate_thz[:, n % 2, :], "g1": gate_th1}[kind]
                    back = 2 if kind == "z" else 1
                    if n >= back:
                        wait_done_upto(act, GATES[n - back])
                    A.activation(dst, bank_of(stage)[:, 0:count], ACT.Tanh, scale=0.5).then_inc(gate_tanh, 1)
                elif kind in ("q", "k1", "q1"):
                    n = HEADU[stage]
                    t = a[-1]
                    wait_unit(act, stage)
                    if kind == "q":
                        if t >= 2:
                            act.wait_ge(tr_ready, TR[("qtr", t - 2)] + 1)
                        buf, sq = qk[:, t % 2, :], qk_sq
                        link(A.copy(buf[:, A_W:640], kraw[:, t, :]))
                        A.copy(buf[:, 0:A_W], bank_of(stage)).then_inc(done_sem(stage), 1)
                    else:
                        buf, sq = (k1v if kind == "k1" else q1v)[:, t, a[0] * SLAB:(a[0] + 1) * SLAB], sq1
                        if stage == ("k1", 0, 0):
                            act.wait_ge(pads_ready, 2)
                        A.copy(buf, bank_of(stage)).then_inc(done_sem(stage), 1)
                    wait_done(act, stage)
                    if n >= 1:
                        act.wait_ge(head_ss, n)
                    A.activation(sq, buf, ACT.Square).then_inc(head_sq, 1)
                elif kind == "qtr":
                    t = a[0]
                    if t == 0:
                        act.wait_ge(pads_ready, 1)
                    act.wait_ge(tr_ready, TR[stage] + 1)
                    src = pair(TR[stage])
                    at_ = slice(t * P, (t + 1) * P)
                    A.copy(qT[:, :, at_], src[:, 0:512].rearrange("p (i t) -> p i t", i=4))
                    A.copy(kpad[0:HD, 0, at_], src[0:HD, 512:640])
                    A.copy(kpad[HD:P, 1, at_], src[HD:P, 512:640]).then_inc(tr_done, 1)
                elif kind == "score":
                    t, g, i = a
                    n = SCORE[stage]
                    r, h, first = n % 8, 4 * g + i, 512 - len(local_tiles(t)) * P
                    act.wait_ge(nmax_ready, n + 1)
                    A.activation(esink[:, r:r + 1], sink[:, h:h + 1], ACT.Exp, bias=nmax[:, r:r + 1])
                    A.activation(prob[:, n % 2, first:768], pair(n)[:, first:768], ACT.Exp, bias=nmax[:, r:r + 1],
                                 scale=SCALE, accum_out=rsum[:, r:r + 1]).then_inc(prob_ready, 1)
                elif kind == "ptr":
                    t, g, i = a
                    n = SCORE[("score",) + a]
                    act.wait_ge(pt_ready, n + 1)
                    nb = len(local_tiles(t)) + NC
                    group = at("pv", t, g)
                    if i == 0 and group > 1:
                        wait_unit(act, PVS[group - 2])
                    A.copy(probT[:, 0:nb, i, :], pt_bank[:, 0:nb * P].rearrange("p (b t) -> p b t", b=nb)
                           ).then_inc(pt_done, 1)
                elif kind == "ynorm":
                    t = a[0]
                    act.wait_ge(gated_y, 2 * NT)
                    if t >= 1:
                        act.wait_ge(y_sq, t)
                    else:
                        act.wait_ge(pt_done, len(SCORE))
                        wait_unit(act, PVS[-1])
                    A.activation(prob_junk, yacc[:, t, :], ACT.Square, scale=0.5, accum_out=ss_y[:, t:t + 1]
                                 ).then_inc(y_sq, 1)
                elif kind == "ytr":
                    k, s = a
                    if s == 1:
                        wait_unit(act, stage)
                        A.activation(hT[:, k, SEQ:TOK], bank_of(stage)[:, 0:CTX], ACT.Copy,
                                     scale=vec2[:, ROW_SSM + k:ROW_SSM + k + 1]).then_inc(done_sem(stage), 1)
                elif kind == "xres":
                    act.wait_ge(xdt_ready, len(STEPS))
                    act.wait_ge(xw_ready, len(STEPS) - 2)
                    for t in range(NT):
                        src = x_in[t * P:(t + 1) * P, :] if t < NX else ctx_in[(t - NX) * P:(t - NX + 1) * P, :]
                        act.dma_start(xin[:, t, :], src).then_inc(xres_in, 16)
                elif kind == "gates":
                    layer = a[0]
                    act.wait_ge(mod_stored, 16 * at("mod", 1, 5))
                    if layer == 0:
                        act.wait_ge(st_done, len(STATEU))
                        act.wait_ge(seg_done[0], len([s for s in SEGU.values() if s % 2 == 0]))
                        act.wait_ge(seg_done[1], len([s for s in SEGU.values() if s % 2 == 1]))
                        for r in range(2):
                            act.dma_start(gate_bc[:, r, :], mod_dram[0, r, 2 * D:3 * D].partition_broadcast(P)
                                          ).then_inc(gate_in, 16)
                        act.dma_start(gate_b, ins["mod_b"][0, 2 * D:3 * D].partition_broadcast(P)
                                      ).then_inc(gate_in, 16)
                        act.dma_start(rope_raw.rearrange("p a t d -> p (a t d)"), ins["rope"]).then_inc(rope_in, 16)
                    else:
                        wait_unit(act, ("hk", C_HEADS - 1, 1))
                        act.dma_start(gate_bc1, mod_dram[1, 0, 2 * D:3 * D].partition_broadcast(P)
                                      ).then_inc(gate1_in, 16)
                        act.dma_start(gate_b1, ins["mod_b"][1, 2 * D:3 * D].partition_broadcast(P)
                                      ).then_inc(gate1_in, 16)
                elif kind in ("hq", "hk"):
                    h = a[0]
                    wait_unit(act, stage)
                    bank = bank_of(stage)
                    if kind == "hq":
                        if h == 0:
                            act.wait_ge(pads_ready, 2)
                        else:
                            act.wait_ge(sc_ready, SC1[("sc1", h - 1, NX - 1, 1)] + 1)
                        A.copy(qpad[0:HD, 0, :], bank[0:HD, :])
                        A.copy(qpad[HD:P, 1, :], bank[HD:P, :]).then_inc(done_sem(stage), 1)
                    else:
                        lo, hi = ((0, SEQ), (SEQ, TOK))[a[1]]
                        A.copy(kT1[:, lo:hi], bank[:, 0:hi - lo]).then_inc(done_sem(stage), 1)
                elif kind == "v1":
                    if a == (0, 0):
                        act.wait_ge(lam_ready, 1)
                        A.activation(lam_e[:, 2:4], lam_e[:, 0:2], ACT.Exp).then_inc(lam_exp, 1)
                    wait_unit(act, stage)
                    A.copy(v1v[:, a[1], a[0] * SLAB:(a[0] + 1) * SLAB], bank_of(stage)).then_inc(done_sem(stage), 1)
                elif kind == "sc1":
                    h, t, c = a
                    n = SC1[stage]
                    r = n % 8
                    act.wait_ge(nmax1, n + 1)
                    if n >= 2:
                        act.wait_ge(pt1_ready, n // 2)
                    A.activation(prob1[:, c, :], pair(n)[:, 0:TOK], ACT.Exp, bias=nmax[:, r:r + 1], scale=SCALE,
                                 accum_out=rsum[:, r:r + 1]).then_inc(prob1_ready, 1)
                elif kind == "ptr1":
                    n = at(*stage) - 1
                    act.wait_ge(pt1_ready, n + 1)
                    if n >= 1:
                        wait_unit(act, PV1S[n - 1])
                    A.copy(probT1, pt_bank[:, 0:TOK].rearrange("p (b t) -> p b t", b=NT)).then_inc(pt1_done, 1)
                elif kind == "pv1":
                    h, t = a
                    wait_unit(act, stage)
                    if at(*stage) > 1:
                        act.wait_ge(o_sq, at(*stage) - 1)
                    A.activation(le, bank_of(stage)[:, 0:P], ACT.Square,
                                 accum_out=ss_o[:, t * 8 + h:t * 8 + h + 1]).then_inc(o_sq, 1)
                elif kind == "otr":
                    h = a[0]
                    if h % 2 == 1:
                        wait_unit(act, stage)
                        A.activation(hT[:, h, 0:SEQ], bank_of(stage), ACT.Copy, scale=head_gain
                                     ).then_inc(done_sem(stage), 1)
                if stage == ("norm", 1, NT - 1):
                    act.dma_start(rope_raw1.rearrange("p a t d -> p (a t d)"), ins["rope"]).then_inc(rope1_in, 16)
                    act.dma_start(lam_p, ins["od_lambda"][0].rearrange("a d -> (a d)").partition_broadcast(P)
                                  ).then_inc(lam_in, 16)

        @block.gpsimd
        def _(pool):
            link = chained(pool, pool_chain)
            G = nc.gpsimd
            for t in range(NT):
                src = x_in[t * P:(t + 1) * P, :] if t < NX else ctx_in[(t - NX) * P:(t - NX + 1) * P, :]
                pool.dma_start(xin[:, t, :], src).then_inc(x_in_s[t], 16)
            for dst, src in ((qkw[:, 0:64], ins["ev_q_norm"][0]), (qkw[:, 64:128], ins["ev_k_norm"][0]),
                             (qkw[:, 128:192], ins["od_q_norm"][0]), (qkw[:, 192:256], ins["od_k_norm"][0]),
                             (sink, ins["ev_sink"][0]), (dtb, ins["ev_dt_bias"][0].rearrange("a h -> (a h)")),
                             (alog, ins["ev_a_log"][0].rearrange("a h -> (a h)")), (dskip, ins["ev_d_skip"][0])):
                pool.dma_start(dst, src.partition_broadcast(P)).then_inc(bc_in, 16)
            pool.wait_ge(pool_start, 1)

            def inverse_root(dst, src, count):
                link(G.tensor_scalar(dst, src, 1.0 / count, EPS, ALU.mult, ALU.add))
                return G.tensor_tensor(dst, dst, neg_half[:, 0:dst.shape[1]], ALU.pow)

            for stage in STAGES:
                kind, a = stage[0], stage[1:]
                if kind == "norm":
                    n = a[0] * NT + a[1]
                    pool.wait_ge(sq_ready, at(*stage))
                    inverse_root(rs_x[:, n:n + 1], ss_x[:, n:n + 1], D).then_inc(rstd_ready, 1)
                elif kind in ("q", "k1", "q1"):
                    n = HEADU[stage]
                    groups = 10 if kind == "q" else 8
                    pool.wait_ge(head_ss, n + 1)
                    if n >= 1:
                        pool.wait_ge(qk_ready, n)
                    inverse_root(rs_h[:, 0:groups], ss_h[:, 0:groups], HD).then_inc(head_rstd, 1)
                elif kind == "ynorm":
                    t = a[0]
                    pool.wait_ge(y_sq, t + 1)
                    inverse_root(rs_y[:, t:t + 1], ss_y[:, t:t + 1], B_INNER).then_inc(y_rstd, 1)
                elif kind == "hnorm":
                    t = a[0]
                    pool.wait_ge(o_sq, TOTAL["pv1"])
                    inverse_root(rs_o[:, t * 8:(t + 1) * 8], ss_o[:, t * 8:(t + 1) * 8], C_V).then_inc(o_rstd, 1)
                elif kind == "cb":
                    d, c = a
                    step = STEP[a]
                    if step == 0:
                        pool.wait_ge(tr_done, sum(1 for s in TR if s[0] == "xtr"))
                        wait_done_upto(pool, ("dt", 1))
                        pool.wait_ge(dta_ready, 1)
                    if step >= 2:
                        pool.wait_ge(intra_ready, 4 * (step - 1))
                    x3 = xs[:, c, :].rearrange("p (h d) -> p h d", h=B_HEADS)
                    cut = slice(c * 16, (c + 1) * 16)
                    dt_c = dt_v[:, d * 96:(d + 1) * 96][:, cut].unsqueeze(2).to_broadcast([P, B_HEADS, HD])
                    we = decay[:, (2 * d + 1) * 96:(2 * d + 2) * 96][:, cut].unsqueeze(2).to_broadcast([P, B_HEADS, HD])
                    if d == 1:
                        G.tensor_tensor(yacc[:, c, :].rearrange("p (h d) -> p h d", h=B_HEADS), x3,
                                        dskip.unsqueeze(2).to_broadcast([P, B_HEADS, HD]), ALU.mult)
                    xd = xdt[:, step % 2, :].rearrange("p (h d) -> p h d", h=B_HEADS)
                    G.tensor_tensor(xd, x3, dt_c, ALU.mult).then_inc(xdt_ready, 1)
                    if a not in LAST_STEP:
                        n = STATEU.get(("state",) + STEPS[step - 1] + (1,)) if step else None
                        if n is not None:
                            pool.wait_ge(st_ready, n + 1)
                        pool.wait_ge(xdt_ready, step + 1)
                        G.tensor_tensor(xw.rearrange("p (h d) -> p h d", h=B_HEADS), xd, we, ALU.mult
                                        ).then_inc(xw_ready, 1)
                elif kind == "seg":
                    d, c, q = a
                    n = SEG[stage]
                    if n >= 2:
                        pool.wait_ge(seg_ready, SEGU[SEGS_[n - 2]] + 1)
                    first = d * 96 + c * 16 + 4 * q
                    G.tensor_tensor(tri_v[:, n % 2, :].rearrange("p (h t) -> p h t", h=4),
                                    (le, ge)[d].unsqueeze(1).to_broadcast([P, 4, P]),
                                    dta_v[:, first:first + 4].unsqueeze(2).to_broadcast([P, 4, P]), ALU.mult
                                    ).then_inc(tri_ready, 1)


_INS = ["x", "c", "ctx", "c_ctx", "mod_w", "mod_b", "norm_w", "ev_w_in", "ev_w_out", "ev_q_norm", "ev_k_norm",
        "ev_sink", "ev_conv_w", "ev_conv_b", "ev_dt_bias", "ev_a_log", "ev_d_skip", "ev_ssm_norm", "od_w_in",
        "od_w_out", "od_q_norm", "od_k_norm", "od_lambda", "od_head_norm"]


def kernel(**inputs):
    import numpy as _np
    import concourse.bacc as _bacc
    from concourse import mybir as _mybir
    from concourse.bass_utils import run_bass_kernel_spmd as _run

    nc = _bacc.Bacc("TRN2", target_bir_lowering=False, num_devices=1)
    arrays, aps = {}, {}
    data = {name: _np.ascontiguousarray(inputs[name]) for name in _INS}
    data["tri"] = triangles()
    data["rope"] = rope_tables()
    for name, a in data.items():
        arrays[f"in_{name}_dram"] = a
        aps[name] = nc.dram_tensor(f"in_{name}_dram", a.shape, _mybir.dt.from_np(a.dtype), kind="ExternalInput").ap()
    out = nc.dram_tensor("out_0_dram", (1, SEQ, D), _mybir.dt.float32, kind="ExternalOutput").ap()
    build(nc, aps, out)
    r = _run(nc, [arrays], core_ids=[0])
    return r.results[0]["out_0_dram"]
```

```python
from contextlib import ExitStack
import math

import numpy as np
import concourse.bass as bass
from concourse import mybir

P = 128
D = 1024
KD = D // P
SEQ, CTX = 512, 256
NX, NC = SEQ // P, CTX // P
NT = NX + NC
TOK = SEQ + CTX
HD = 64
SLAB = 512
RING = 3
EPS = 1e-6
GRID_W = 64
ROPE_BASE = 10000.0

A_HEADS, A_KV = 8, 2
A_GROUP = A_HEADS // A_KV
A_W = A_HEADS * HD
A_KVW = A_KV * HD
B_HEADS, B_G, B_N = 16, 2, 128
B_INNER = D
TAPS = 5
XBC = B_INNER + 2 * B_G * B_N
FT = XBC // P
COL_Q, COL_K = 0, A_W
COL_V = COL_K + A_KVW
COL_GA = COL_V + A_KVW
COL_Z = COL_GA + A_W
COL_XBC = COL_Z + B_INNER
COL_DT = COL_XBC + XBC
KVDT = 2 * A_KVW + 2 * B_HEADS
EVEN_MIX = A_W + B_INNER
KM = EVEN_MIX // P
C_HEADS, C_V = 8, 128
LAMBDA_INIT = 0.8 - 0.6 * math.exp(-0.3)
SCALE = HD ** -0.5
NEG = -1e30

F32 = mybir.dt.float32
BF16 = mybir.dt.bfloat16
ALU = mybir.AluOpType
ACT = mybir.ActivationFunctionType
AXX = mybir.AxisListType.X

ROW_C, ROW_CC, ROW_NORM, ROW_MODB = 0, 8, 16, 32
ROWS1 = 64
ROW_TAP, ROW_CONVB, ROW_SSM, ROW_HEAD = 0, TAPS * FT, TAPS * FT + FT, TAPS * FT + FT + KD
ROWS2 = ROW_HEAD + 1

SEGS = (("x", 0, SEQ, NX), ("c", SEQ, CTX, NC))


Z_PARTS = 4


def stages_layer0():
    st = [("params", 0), ("params", 1)]
    st += [("mod", 0, s) for s in range(3)]
    st += [("norm", 0, t) for t in range(NT)]
    st += [("mod", 0, 3), ("modcol", 0)]
    st += [("trn", 0, k, 0) for k in range(KD)] + [("trn", 0, k, 1) for k in range(0, KD, 2)]
    conv_order = [8, 9, 10, 11, 0, 1, 2, 3, 4, 5, 6, 7]
    for n, f in enumerate(conv_order):
        if n >= 1:
            st.append(("silu", conv_order[n - 1]))
        st += [("xbc", f, 0), ("xbc", f, 1)]
        if n >= 1 and conv_order[n - 1] not in (10, 11):
            st.append(("xtr", conv_order[n - 1]))
    st += [("kvdt", 0), ("silu", conv_order[-1]), ("kvdt", 1), ("xtr", conv_order[-1])]
    st += [("kvdt", t) for t in range(2, NT)]
    fill = [("ga", f, s) for f in range(4) for s in range(2)]
    fill += [("mod", 0, 4), ("mod", 0, 5)] + [("mod", 1, s) for s in range(6)]
    st += [("dtv",), fill.pop(0), ("dt", 0), ("dt", 1), fill.pop(0), fill.pop(0)]
    steps = [(1, 5), (1, 4), (1, 3), (1, 2), (1, 1), (1, 0), (0, 4), (0, 5), (0, 0), (0, 1), (0, 2), (0, 3)]
    quads = [(d, c, q) for d, c in steps for q in (1, 0, 3, 2)]
    for n in range(len(quads) + 2):
        if n < len(quads):
            d, c, q = quads[n]
            if n % 4 == 0:
                st.append(("cb", d, c))
            st.append(("seg", d, c, q))
        if n >= 2:
            d, c, q = quads[n - 2]
            st.append(("intra", d, c, q))
            if q % 2 == 0:
                st.append(("ysum", d, c, q // 2))
        if n < len(quads) and n % 4 in (1, 2):
            st.append((("inter", "state")[n % 4 - 1],) + quads[n][:2])
        if n % 3 == 1 and fill:
            st.append(fill.pop(0))
    st += fill + [("xres",), ("gates", 0), ("modin", 1)]
    fill = [("z", t, n) for n in range(2) for t in range(NT)]
    for t in range(NT):
        st += [("q", t)]
        if t == 1:
            st.append(fill.pop(0))
        if t >= 2:
            st += [("qtr", t - 2)]
    st += [fill.pop(0), ("qtr", NT - 2), ("modcol", 1), fill.pop(0), ("qtr", NT - 1)]
    fill = [part for z in fill for part in [("zpart",) + z[1:] + (j,) for j in range(Z_PARTS - 1)] + [z]]
    after_z = [("ysq", 0)] + [s for t in range(1, NT) for s in (("ysq", t), ("ynorm", t - 1))]
    after_z += [("ynorm", NT - 1)] + [("ytr", k, s) for k in range(KD) for s in range(2)]
    heads = [(t, g, i) for t in (4, 5, 0, 1, 2, 3) for g in range(A_KV) for i in range(A_GROUP)]
    for n in range(len(heads) + 3):
        if n < len(heads):
            st.append(("score",) + heads[n])
        if n >= 3 and heads[n - 3][2] == A_GROUP - 1:
            st.append(("pv",) + heads[n - 3][:2])
        if fill:
            st.append(fill.pop(0))
        if 2 <= n < len(heads) + 2:
            st.append(("ptr",) + heads[n - 2])
        if n < len(heads):
            st.append(("expo",) + heads[n])
        if 1 <= n <= len(heads):
            st.append(("pnorm",) + heads[n - 1])
        if not fill and after_z:
            st.append(after_z.pop(0))
            if after_z and after_z[0][0] in ("ytr", "ynorm"):
                st.append(after_z.pop(0))
    st += after_z + [("gatesum", 0)]
    st += [("out0", 0, t) for t in range(NT)]
    for t in range(NT):
        st += [("out0", 1, t)]
        if t < NT - 1:
            st += [("norm", 1, t)]
    return st


def stages_layer1():
    st = [("trn", 1, k, 0) for k in range(4)] + [("norm", 1, NT - 1)]
    st += [("trn", 1, k, 0) for k in range(4, KD)] + [("trn", 1, k, 1) for k in range(0, KD, 2)]
    st += [("k1", n, t) for n in range(2) for t in range(NT)]
    st += [("v1", n, t) for n in range(2) for t in range(NT)]
    st += [("q1", n, t) for n in range(2) for t in range(NX)]
    fill = [("g1", n, t) for n in range(2) for t in range(NX)]
    work = [(h, t) for h in range(C_HEADS) for t in range(NX)]
    late = []
    st += [("hk", 0, 1), ("hq", 0), ("hk", 0, 0)]
    for n in range(len(work) + 2):
        if n < len(work):
            st.append(("sc1",) + work[n] + (0,))
        if n >= 2:
            st.append(("ptr1",) + work[n - 2])
        if n < len(work):
            h, t = work[n]
            st.append(("sc1", h, t, 1))
            if t == NX - 1 and h < C_HEADS - 1:
                st += [("hk", h + 1, 1), ("hq", h + 1), ("hk", h + 1, 0)]
            st.append(("exp1", h, t))
        if 1 <= n <= len(work):
            st.append(("comb1",) + work[n - 1])
        if fill and (n < 4 or n % 2 == 0):
            st.append(fill.pop(0))
        if n >= 2:
            st.append(("pv1",) + work[n - 2])
            if late and not fill:
                st.append(late.pop(0))
            if work[n - 2][1] == NX - 1:
                late += [("hnorm", work[n - 2][0]), ("otr", work[n - 2][0])]
            if work[n - 2] == (C_HEADS - 1, 1):
                st.append(("gates", 1))
    st += late + [("gatesum", 1)]
    st += [("out1", n, t) for n in range(2) for t in range(NX)]
    return st


STAGES = stages_layer0() + stages_layer1()


def count_stages():
    seen, out = {}, {}
    for s in STAGES:
        seen[s[0]] = seen.get(s[0], 0) + 1
        out[s] = seen[s[0]]
    return out, seen


AT, TOTAL = count_stages()
assert len(AT) == len(STAGES)


def at(*stage):
    return AT[stage]


UNIT_STAGES = ("params", "mod", "modcol", "xbc", "kvdt", "dt", "q", "ga", "z", "pv", "ytr", "out0",
               "k1", "v1", "q1", "g1", "hq", "hk", "pv1", "otr", "out1")
UNITS = [s for s in STAGES if s[0] in UNIT_STAGES]
UNIT = {s: n for n, s in enumerate(UNITS)}


def slabs_of(stage):
    kind = stage[0]
    if kind == "mod":
        return [stage]
    if kind == "xbc":
        return [("xbc", stage[1] // 4)]
    if kind in ("kvdt", "q", "ga"):
        return [(kind,)]
    if kind == "z":
        return [("z", stage[2])]
    if kind == "out0":
        return [("out0", stage[1], 0), ("out0", stage[1], 1)]
    if kind in ("k1", "v1", "q1", "g1", "out1"):
        return [(kind, stage[1])]
    return []


SLABS, LAST_USE = [], {}
for _s in UNITS:
    for _k in slabs_of(_s):
        if _k not in LAST_USE:
            SLABS.append(_k)
        LAST_USE[_k] = UNIT[_s]
SLAB_NO = {k: n for n, k in enumerate(SLABS)}
SLAB_DMAS = [2 if k == ("kvdt",) else 1 for k in SLABS]


def slab_landed(n):
    return 16 * sum(SLAB_DMAS[m] for m in range(n % RING, n + 1, RING))


def ordinal(kinds):
    return {s: n for n, s in enumerate([s for s in STAGES if s[0] in kinds])}


TR = ordinal(("xtr", "qtr"))
TRN = ordinal(("trn",))
TRNS = len(TRN) // 2
SEGU = ordinal(("cb", "seg"))
FIRST_STEP = ((1, NT - 1), (0, NX))
LAST_STEP = ((1, 0), (0, NX - 1))
STATEU = {}
for _s in STAGES:
    if (_s[0] == "inter" and _s[1:] not in FIRST_STEP) or (_s[0] == "state" and _s[1:] not in LAST_STEP):
        for _g in range(B_G):
            STATEU[_s + (_g,)] = len(STATEU)
MOD_ON_CHIP = [(0, s) for s in range(4)]
MOD_STORE = {s: n for n, s in enumerate([s for s in STAGES if s[0] == "mod" and s[1:] not in MOD_ON_CHIP])}
STEPS = [s[1:] for s in STAGES if s[0] == "cb"]
STEP = {s: n for n, s in enumerate(STEPS)}
SEG = ordinal(("seg",))
SCORE = ordinal(("score",))
SC1 = ordinal(("sc1",))
HEADU = ordinal(("q", "k1", "q1"))
HEADN = {s: n - NT for s, n in HEADU.items()}
GATE = ordinal(("ga", "z", "g1"))
GATES = list(GATE)
PVS = [s for s in STAGES if s[0] == "pv"]
PV1S = [s for s in STAGES if s[0] == "pv1"]
SEGS_ = list(SEG)


def rope_tables():
    n_freq = HD // 4
    tok = np.arange(SEQ)
    inv = (np.float32(ROPE_BASE) ** (-np.arange(n_freq, dtype=np.float32) / n_freq)).astype(np.float32)
    row = (tok // GRID_W).astype(np.float32)[:, None] * inv
    col = (tok % GRID_W).astype(np.float32)[:, None] * inv
    ang = np.concatenate([row, row, col, col], -1).astype(np.float32)
    cos, sin = np.cos(ang), np.sin(ang)
    sign = np.where((np.arange(HD) // n_freq) % 2 == 0, -1.0, 1.0).astype(np.float32)
    both = np.stack([cos, sin * sign])
    return np.ascontiguousarray(both.reshape(2, NX, P, HD).transpose(2, 0, 1, 3).reshape(P, 2 * NX * HD)
                                ).astype(np.float32)


def triangles():
    k, j = np.arange(P)[:, None], np.arange(P)[None, :]
    parts = [k == j, k <= j, k >= j, k > j, k < j]
    parts = [np.asarray(m, np.float32) for m in parts]
    parts += [np.where(j >= k, 0.0, NEG), np.where(j <= k, 0.0, NEG)]
    return np.ascontiguousarray(np.concatenate(parts, 1)).astype(np.float32)


def build(nc, ins, out):
    x_in, ctx_in = ins["x"].rearrange("a t d -> (a t) d"), ins["ctx"].rearrange("a t d -> (a t) d")
    w_even, w_even_out = ins["ev_w_in"][0], ins["ev_w_out"][0]
    w_odd, w_odd_out = ins["od_w_in"][0], ins["od_w_out"][0]
    out_v = out.rearrange("a t d -> (a t) d")
    mod_dram = nc.dram_tensor("mod_rows_dram", (2, 2, 3 * D), F32, kind="Internal").ap()

    with ExitStack() as ctx:
        def sb(name, width, dt=F32):
            return ctx.enter_context(nc.sbuf_tensor(name, [P, width], dt))[:, :]

        def sem(name):
            return ctx.enter_context(nc.semaphore(name))

        ps = ctx.enter_context(nc.psum_tensor("ps", [P, 8, 512], F32))[:, :, :]

        ring = sb("ring", RING * KD * SLAB)
        hT = sb("hT", KD * TOK).rearrange("p (k t) -> p k t", k=KD)
        xs_all = sb("xs_all", NT * D)
        y_all = sb("y_all", NT * D)
        POOL = 19456
        pool_mem = sb("pool_mem", POOL)

        def carve(start, width):
            assert start + width <= POOL, (start, width)
            return pool_mem[:, start:start + width]

        consts = sb("consts", 5 * P)
        ones = sb("ones", P)
        edges = sb("edges", 3 * P, BF16)
        vec1, vec2 = sb("vec1", ROWS1), sb("vec2", ROWS2)
        halftap = sb("halftap", ROW_SSM)
        silu_c = sb("silu_c", 16)
        mod_cols = sb("mod_cols", 32)
        gain_cols = sb("gain_cols", 16)
        bc = sb("bc", 448)
        qkw = bc[:, 0:256]
        sink, dtb, alog, dskip = bc[:, 256:264], bc[:, 264:296], bc[:, 296:328], bc[:, 328:344]
        nsink, lam = bc[:, 344:352], bc[:, 352:356]
        dtv = sb("dtv", 2 * 192)
        dt_v, dta_v = dtv[:, 0:192], dtv[:, 192:384]
        decay = sb("decay", 384)
        cdec = sb("cdec", 192)
        stat = sb("stat", 192)

        ident, le, ge, gt, lt = (consts[:, n * P:(n + 1) * P] for n in range(5))
        identb, edge_lo, edge_hi = (edges[:, n * P:(n + 1) * P] for n in range(3))

        bct = carve(0, 4 * TOK).rearrange("p (f t) -> p f t", f=4)
        btok = carve(3072, NT * 2 * P).rearrange("p (t g n) -> p t g n", t=NT, g=2)
        gaT = carve(4608, 4 * TOK).rearrange("p (f t) -> p f t", f=4)
        qT = carve(7680, 4 * TOK).rearrange("p (i t) -> p i t", i=4)
        kpad = carve(10752, 2 * TOK).rearrange("p (g t) -> p g t", g=2)
        vdup = carve(12288, NT * 2 * P).rearrange("p (t g u d) -> p t g u d", t=NT, g=2, u=2)
        kraw = carve(13824, NT * P).rearrange("p (t c) -> p t c", t=NT)
        S0 = 14592
        conv = carve(S0, 3 * TOK).rearrange("p (r t) -> p r t", r=3)
        conv_th = carve(S0 + 2304, 2 * TOK).rearrange("p (r t) -> p r t", r=2)
        xsT = carve(7680, 2 * TOK).rearrange("p (r t) -> p r t", r=2)
        dt_tmp = carve(S0, 6 * 192).rearrange("p (r n) -> p r n", r=6)
        dt_raw = carve(9216, 192)
        xdt = carve(7680, 2 * D).rearrange("p (r n) -> p r n", r=2)
        xw = carve(9728, D)
        hst = carve(10752, D)
        cbm = carve(11776, 512).rearrange("p (r g t) -> p r g t", r=2, g=2)
        tri_v = carve(S0, 2 * 512).rearrange("p (r n) -> p r n", r=2)
        emat = carve(S0 + 1024, 3 * 512).rearrange("p (r n) -> p r n", r=3)
        y_in = carve(S0 + 2560, D).rearrange("p (g n) -> p g n", g=2)
        gate_th = carve(S0 + 3584, 512)
        mod_row = carve(S0 + 4096, 512)
        mod_blk = carve(S0 + 4608, P)[0:32, :]
        mod_rows0 = carve(S0, 2 * D)[0:2, :]
        edges_f32 = carve(2 * P, 2 * P)
        qk = carve(S0, 2 * 640).rearrange("p (r n) -> p r n", r=2)
        qk_sq = carve(S0 + 1280, 640)
        rope_a, rope_b = carve(S0 + 1920, 640), carve(S0 + 2560, 640)
        rope_t = carve(S0 + 3200, 1024).rearrange("p (w a t d) -> p w a t d", w=2, a=2, t=NX)
        rope_raw = carve(3072, 512).rearrange("p (a t d) -> p a t d", a=2, t=NX)
        prob = carve(S0, 2 * 768).rearrange("p (r n) -> p r n", r=2)
        probT = carve(S0 + 1536, 2560).rearrange("p (b i t) -> p b i t", b=5, i=4)
        zg = carve(3072, 512)
        gate_thz = carve(3584, 2 * 512).rearrange("p (r n) -> p r n", r=2)
        y_junk = carve(3584, D)
        gate_bc = carve(0, 2 * D).rearrange("p (s n) -> p s n", s=2)
        gate_b = carve(2048, D)
        res_tmp = carve(S0, 2 * 512).rearrange("p (r n) -> p r n", r=2)
        k1v = carve(0, NT * D).rearrange("p (t n) -> p t n", t=NT)
        q1v = carve(6144, NX * D).rearrange("p (t n) -> p t n", t=NX)
        g1v = carve(10240, NX * D).rearrange("p (t n) -> p t n", t=NX)
        L1 = 14336
        qpad = carve(L1, 2 * SEQ).rearrange("p (c t) -> p c t", c=2)
        kT1 = carve(L1 + 1024, TOK)
        probT1 = carve(L1 + 1792, 768).rearrange("p (b t) -> p b t", b=NT)
        sq1 = carve(L1 + 2560, 512)
        rope_a1, rope_b1 = carve(L1 + 3072, 512), carve(L1 + 3584, 512)
        rope_t1 = carve(L1 + 4096, 1024).rearrange("p (w a t d) -> p w a t d", w=2, a=2, t=NX)
        rope_raw1 = carve(0, 512).rearrange("p (a t d) -> p a t d", a=2, t=NX)
        gate_th1 = xs_all[:, NX * D + 1536:NX * D + 2048]
        prob1 = [m.rearrange("p (c n) -> p c n", c=2)
                 for m in (xs_all[:, NX * D:NX * D + 1536], carve(L1 + 2560, 1536))]
        gate_bc1, gate_b1 = carve(0, D), carve(D, D)
        res_tmp1 = carve(2 * D, 2 * 512).rearrange("p (r n) -> p r n", r=2)

        xin = xs_all.rearrange("p (t n) -> p t n", t=NT)
        xs = xin
        x1 = xin
        xhat = y_all.rearrange("p (t n) -> p t n", t=NT)
        yacc = xhat
        v1v = xhat
        junk = hT.rearrange("p k t -> p (k t)")[:, 0:D]
        junk1 = carve(7680, D)
        rows1 = carve(0, P)[0:ROWS1, :]
        rows2 = carve(P, P)[0:ROWS2, :]

        ss_x, rs_x = stat[:, 0:12], stat[:, 12:24]
        ss_y, rs_y = stat[:, 24:30], stat[:, 30:36]
        ss_h, rs_h = stat[:, 36:48], stat[:, 48:60]
        ss_o, rs_o = stat[:, 60:92], stat[:, 92:124]
        rmax, rsum, rinv = stat[:, 124:132], stat[:, 132:140], stat[:, 140:148]
        nmax, esink = stat[:, 148:156], stat[:, 156:164]
        neg_half = stat[:, 164:180]
        lam_e = stat[:, 180:184]
        lam_p = dtv[:, 0:256]
        head_gain = stat[:, 184:185]
        neg_lam = stat[:, 185:186]

        slab_in = [sem(f"slab_in{n}") for n in range(RING)]
        unit_ready = sem("unit_ready")
        unit_done = [sem(f"unit_done{n}") for n in range(2)]
        const_in, row_in, bc_in, lam_in, rope_in, rope1_in = (sem(n) for n in (
            "const_in", "row_in", "bc_in", "lam_in", "rope_in", "rope1_in"))
        x_in_s = [sem(f"x_in{t}") for t in range(NT)]
        xres_in, gate_in, gate1_in = sem("xres_in"), sem("gate_in"), sem("gate1_in")
        mod_stored, mod_rows = sem("mod_stored"), sem("mod_rows")
        out_stored = sem("out_stored")
        edges_ready, tanh_c, silu_c_ready, cols_ready = (sem(n) for n in (
            "edges_ready", "tanh_c", "silu_c_ready", "cols_ready"))
        sq_ready, rstd_ready, xhat_ready = sem("sq_ready"), sem("rstd_ready"), sem("xhat_ready")
        conv_tanh, silu_ready, tr_ready, tr_done = (sem(n) for n in (
            "conv_tanh", "silu_ready", "tr_ready", "tr_done"))
        dt_exp, dt_dve, dta_ready = sem("dt_exp"), sem("dt_dve"), sem("dta_ready")
        xdt_ready, xw_ready, tri_ready = sem("xdt_ready"), sem("xw_ready"), sem("tri_ready")
        seg_ready, emat_ready, intra_ready = sem("seg_ready"), sem("emat_ready"), sem("intra_ready")
        seg_done = [sem(f"seg_done{n}") for n in range(2)]
        st_ready, st_done, h_ready, intra_done = (sem(n) for n in ("st_ready", "st_done", "h_ready", "intra_done"))
        trn_ready, trn_done = sem("trn_ready"), [sem(f"trn_done{n}") for n in range(2)]
        gate_tanh, head_sq, head_ss, head_rstd, qk_ready = (sem(n) for n in (
            "gate_tanh", "head_sq", "head_ss", "head_rstd", "qk_ready"))
        score_ready, nmax_ready, prob_ready, probn_ready, pt_ready, pt_done = (sem(n) for n in (
            "score_ready", "nmax_ready", "prob_ready", "probn_ready", "pt_ready", "pt_done"))
        gated_y, y_sq, y_rstd, y_ready, x1_ready = (sem(n) for n in (
            "gated_y", "y_sq", "y_rstd", "y_ready", "x1_ready"))
        gates_ready, pads_ready = sem("gates_ready"), sem("pads_ready")
        o_sq, o_rstd, o_ready, o_gated = sem("o_sq"), sem("o_rstd"), sem("o_ready"), sem("o_gated")
        sc_ready, nmax1, prob1_ready, a_ready, pt1_ready, pt1_done = (sem(n) for n in (
            "sc_ready", "nmax1", "prob1_ready", "a_ready", "pt1_ready", "pt1_done"))
        lam_ready, lam_exp = sem("lam_ready"), sem("lam_exp")
        out_ready = sem("out_ready")
        dve_chain, act_chain, pool_chain = sem("dve_chain"), sem("act_chain"), sem("pool_chain")
        pool_start = sem("pool_start")

        def chained(eng, chain):
            n = [0]

            def link(instr):
                n[0] += 1
                instr.then_inc(chain, 1)
                eng.wait_ge(chain, n[0])
            return link

        def wait_unit(eng, stage):
            eng.wait_ge(unit_ready, UNIT[stage] + 1)

        def wait_done(eng, stage):
            n = UNIT[stage]
            eng.wait_ge(unit_done[n % 2], n // 2 + 1)

        def wait_done_upto(eng, stage):
            n = UNIT[stage]
            for m in (n - 1, n):
                eng.wait_ge(unit_done[m % 2], m // 2 + 1)

        def bank_of(stage):
            return ps[:, UNIT[stage] % 2, :]

        def done_sem(stage):
            return unit_done[UNIT[stage] % 2]

        def pair(n):
            b = 2 + 2 * (n % 2)
            return ps[:, b:b + 2, :].rearrange("p b n -> p (b n)")

        pt_bank = ps[:, 6:8, :].rearrange("p b n -> p (b n)")

        def slab_ap(key):
            n = SLAB_NO[key]
            k = 6 if key[0] == "out0" else KD
            return ring[:, (n % RING) * KD * SLAB:(n % RING) * KD * SLAB + k * SLAB].rearrange(
                "p (k n) -> p k n", k=k)

        def slab_source(key):
            kind = key[0]
            view = lambda w: w.rearrange("(k p) n -> p k n", p=P)
            if kind == "mod":
                return view(ins["mod_w"][key[1]])[:, :, key[2] * SLAB:(key[2] + 1) * SLAB]
            if kind == "xbc":
                return view(w_even)[:, :, COL_XBC + key[1] * SLAB:COL_XBC + (key[1] + 1) * SLAB]
            if kind == "q":
                return view(w_even)[:, :, COL_Q:COL_Q + SLAB]
            if kind == "ga":
                return view(w_even)[:, :, COL_GA:COL_GA + SLAB]
            if kind == "z":
                return view(w_even)[:, :, COL_Z + key[1] * SLAB:COL_Z + (key[1] + 1) * SLAB]
            if kind == "out0":
                return view(w_even_out)[:, 6 * key[2]:6 * key[2] + 6, key[1] * SLAB:(key[1] + 1) * SLAB]
            if kind == "out1":
                return view(w_odd_out)[:, :, key[1] * SLAB:(key[1] + 1) * SLAB]
            first = {"q1": 0, "k1": D, "v1": 2 * D, "g1": 3 * D}[kind] + key[1] * SLAB
            return view(w_odd)[:, :, first:first + SLAB]

        def local_tiles(t):
            return [] if t >= NX else list(range(max(0, t - 1), min(NX - 1, t + 1) + 1))

        block = ctx.enter_context(nc.Block())

        @block.sync
        def _(sp):
            sp.dma_start(consts, ins["tri"][:, 0:5 * P]).then_inc(const_in, 16)
            sp.dma_start(edges_f32, ins["tri"][:, 5 * P:7 * P]).then_inc(const_in, 16)
            r = 0
            for name, count, dst in (("c", 8, rows1), ("c_ctx", 8, rows1), ("norm_w", 16, rows1)):
                src = ins[name]
                src = src.rearrange("a (k p) -> (a k) p", p=P) if len(src.shape) == 2 else \
                    src.rearrange("(k p) -> k p", p=P)
                sp.dma_start(dst[r:r + count, :], src).then_inc(row_in, 16)
                r += count
            for l in range(2):
                sp.dma_start(rows1[ROW_MODB + 16 * l:ROW_MODB + 16 * (l + 1), :],
                             ins["mod_b"][l, 0:2 * D].rearrange("(k p) -> k p", p=P)).then_inc(row_in, 16)
            sp.dma_start(rows2[0:ROW_CONVB, :], ins["ev_conv_w"][0].rearrange("a (k p) -> (a k) p", p=P)
                         ).then_inc(row_in, 16)
            sp.dma_start(rows2[ROW_CONVB:ROW_SSM, :], ins["ev_conv_b"].rearrange("a (k p) -> (a k) p", p=P)
                         ).then_inc(row_in, 16)
            sp.dma_start(rows2[ROW_SSM:ROW_HEAD, :], ins["ev_ssm_norm"].rearrange("a (k p) -> (a k) p", p=P)
                         ).then_inc(row_in, 16)
            sp.dma_start(rows2[ROW_HEAD:ROWS2, :], ins["od_head_norm"]).then_inc(row_in, 16)
            for n, key in enumerate(SLABS):
                if n == 0:
                    continue
                if n >= RING:
                    sp.wait_ge(unit_ready, LAST_USE[SLABS[n - RING]] + 1)
                dst, arrived = slab_ap(key), slab_in[n % RING]
                if key == ("kvdt",):
                    view = w_even.rearrange("(k p) n -> p k n", p=P)
                    sp.dma_start(dst[:, :, 0:2 * A_KVW], view[:, :, COL_K:COL_K + 2 * A_KVW]).then_inc(arrived, 16)
                    sp.dma_start(dst[:, :, 2 * A_KVW:KVDT], view[:, :, COL_DT:COL_DT + 2 * B_HEADS]
                                 ).then_inc(arrived, 16)
                else:
                    sp.dma_start(dst, slab_source(key)).then_inc(arrived, 16)
            for n in range(2):
                for t in range(NX):
                    sp.wait_ge(out_ready, at("out1", n, t))
                    sp.dma_start(out_v[t * P:(t + 1) * P, n * SLAB:(n + 1) * SLAB],
                                 x1[:, t, n * SLAB:(n + 1) * SLAB]).then_inc(out_stored, 16)
            sp.wait_ge(out_stored, 16 * 2 * NX)

        @block.tensor
        def _(pe):
            def begin(stage):
                n = UNIT[stage]
                if n >= 2:
                    pe.wait_ge(unit_done[n % 2], n // 2)
                return ps[:, n % 2, :]

            def slab_landing(key):
                n = SLAB_NO[key]
                pe.wait_ge(slab_in[n % RING], slab_landed(n))
                return slab_ap(key)

            def slabs(stage):
                return [slab_landing(key) for key in slabs_of(stage)]

            def project(stage, width, lhs_of, rhs_of, count):
                bank = begin(stage)
                for k in range(count):
                    mm = pe.matmul(bank[:, 0:width], lhs_of(k), rhs_of(k), start=(k == 0), stop=(k == count - 1))
                mm.then_inc(unit_ready, 1)

            def token_major(stage, t, width=SLAB):
                (w,) = slabs(stage)
                project(stage, width, lambda k: hT[:, k, t * P:(t + 1) * P], lambda k: w[:, k, 0:width], KD)

            def feature_major(stage, f, s):
                (w,) = slabs(stage)
                _, first, count, _ = SEGS[s]
                project(stage, count, lambda k: w[:, k, f * P:(f + 1) * P],
                        lambda k: hT[:, k, first:first + count], KD)

            def turn(stage, blocks):
                bank = begin(stage)
                for j, b in enumerate(blocks):
                    mm = pe.transpose(bank[:, j * P:(j + 1) * P], b, ident)
                mm.then_inc(unit_ready, 1)

            def wait_hT(layer):
                for b in range(2):
                    pe.wait_ge(trn_done[b], (layer + 1) * TRNS // 2)

            for stage in STAGES:
                kind, a = stage[0], stage[1:]
                if kind == "params":
                    rows, count = ((rows1, ROWS1), (rows2, ROWS2))[a[0]]
                    pe.wait_ge(const_in, 32)
                    pe.wait_ge(row_in, 16 * 9)
                    bank = begin(stage)
                    pe.transpose(bank[:, 0:count], rows, ident[0:count, 0:count]).then_inc(unit_ready, 1)
                elif kind == "mod":
                    pe.wait_ge(silu_c_ready, 1)
                    (w,) = slabs(stage)
                    bank = begin(stage)
                    both = silu_c.rearrange("p (r k) -> p k r", r=2)
                    for k in range(KD):
                        mm = pe.matmul(bank[0:2, :], both[:, k, :], w[:, k, :], start=(k == 0), stop=(k == KD - 1))
                    mm.then_inc(unit_ready, 1)
                elif kind == "modcol":
                    if a[0] == 0:
                        wait_done_upto(pe, ("mod", 0, 3))
                        bank = begin(stage)
                        for j in range(2 * KD):
                            mm = pe.transpose(bank[:, 2 * j:2 * j + 2], mod_rows0[:, j * P:(j + 1) * P],
                                              ident[0:2, 0:2])
                        mm.then_inc(unit_ready, 1)
                    else:
                        pe.wait_ge(mod_rows, 16)
                        bank = begin(stage)
                        pe.transpose(bank[:, 0:32], mod_blk, ident[0:32, 0:32]).then_inc(unit_ready, 1)
                elif kind == "trn":
                    layer, k, s = a
                    _, first, _, tiles = SEGS[s]
                    pe.wait_ge(xhat_ready, at("norm", layer, first // P + tiles - 1))
                    n = TRN[stage]
                    if layer == 1:
                        pe.wait_ge(prob_ready, len(SCORE))
                    if n >= 4:
                        pe.wait_ge(trn_done[n % 2], n // 2 - 1)
                    blocks = [(i, first // P + j) for i in range(k, k + 1 + s) for j in range(tiles)]
                    for j, (i, t) in enumerate(blocks):
                        mm = pe.transpose(ps[:, 2 + n % 4, j * P:(j + 1) * P], xhat[:, t, i * P:(i + 1) * P], ident)
                    mm.then_inc(trn_ready, 1)
                elif kind == "xbc":
                    if stage == ("xbc", 8, 0):
                        wait_hT(0)
                    feature_major(stage, a[0] % 4, a[1])
                elif kind in ("xtr", "qtr"):
                    n = TR[stage]
                    if n >= 2:
                        pe.wait_ge(tr_done, n - 1)
                    if kind == "xtr":
                        f = a[0]
                        pe.wait_ge(silu_ready, at("silu", f))
                        src = bct[:, f - 8, :] if f >= 8 else xsT[:, f % 2, :]
                        blocks = [src[:, t * P:(t + 1) * P] for t in range(NT)]
                    else:
                        t = a[0]
                        if t == 0:
                            pe.wait_ge(st_done, len(STATEU))
                            pe.wait_ge(intra_done, 2 * len(STEPS))
                            for b in range(2):
                                pe.wait_ge(seg_done[b], len(SEGU) // 2)
                        pe.wait_ge(qk_ready, t + 1)
                        blocks = [qk[:, t % 2, i * P:(i + 1) * P] for i in range(5)]
                    for j, b in enumerate(blocks):
                        mm = pe.transpose(pair(n)[:, j * P:(j + 1) * P], b, ident)
                    mm.then_inc(tr_ready, 1)
                elif kind == "kvdt":
                    token_major(stage, a[0], KVDT)
                elif kind == "dt":
                    pe.wait_ge(dta_ready, 1)
                    bank = begin(stage)
                    dta = dta_v.rearrange("p (d n) -> p d n", d=2)
                    if a[0] == 0:
                        for j, (m, d) in enumerate(((le, 0), (gt, 0), (ge, 1), (lt, 1))):
                            mm = pe.matmul(bank[:, j * 96:(j + 1) * 96], m, dta[:, d, :], start=(j == 0), stop=True,
                                           skip_group_check=True)
                    else:
                        mm = pe.matmul(bank[:, 0:192], ones, dta_v, start=True, stop=True)
                    mm.then_inc(unit_ready, 1)
                elif kind == "cb":
                    d, c = a
                    n = SEGU[stage]
                    if n == 0:
                        pe.wait_ge(tr_done, sum(1 for s in TR if s[0] == "xtr"))
                    if n >= 2:
                        pe.wait_ge(seg_done[n % 2], n // 2)
                    for g in range(B_G):
                        mm = pe.matmul(ps[:, 2 + n % 2, g * P:(g + 1) * P], bct[:, g, c * P:(c + 1) * P],
                                       bct[:, 2 + g, c * P:(c + 1) * P], start=(g == 0), stop=True,
                                       skip_group_check=True)
                    mm.then_inc(seg_ready, 1)
                elif kind == "seg":
                    d = a[0]
                    n = SEGU[stage]
                    if n >= 2:
                        pe.wait_ge(seg_done[n % 2], n // 2)
                    pe.wait_ge(tri_ready, SEG[stage] + 1)
                    pe.matmul(ps[:, 2 + n % 2, :], (gt, lt)[d], tri_v[:, SEG[stage] % 2, :], start=True, stop=True
                              ).then_inc(seg_ready, 1)
                elif kind in ("inter", "state"):
                    d, c = a
                    if stage + (0,) not in STATEU:
                        continue
                    if kind == "inter":
                        pe.wait_ge(h_ready, STEP[(d, c)] - (d == 0))
                    else:
                        pe.wait_ge(xw_ready, STEP[(d, c)] + 1 - (d == 0))
                    for g in range(B_G):
                        n = STATEU[stage + (g,)]
                        if n >= 2:
                            pe.wait_ge(st_done, n - 1)
                        lhs = bct[:, 2 + g, c * P:(c + 1) * P] if kind == "inter" else btok[:, c, g, :]
                        rhs = (hst if kind == "inter" else xw)[:, g * 512:(g + 1) * 512]
                        pe.matmul(ps[:, (4, 7)[n % 2], :], lhs, rhs, start=True, stop=True).then_inc(st_ready, 1)
                elif kind == "intra":
                    d, c, q = a
                    g, step = q // 2, STEP[(d, c)]
                    if q % 2 == 1 and step > 0:
                        pe.wait_ge(intra_done, 2 * step - 1 + g)
                    pe.wait_ge(emat_ready, SEG[("seg",) + a] + 1)
                    pe.wait_ge(xdt_ready, step + 1)
                    for i in (3, 2, 1, 0):
                        h = 4 * (q % 2) + i
                        left = max(h - 1, 0)
                        mm = pe.matmul(ps[:, 5 + g, left * HD:(h + 1) * HD],
                                       emat[:, SEG[("seg",) + a] % 3, i * P:(i + 1) * P],
                                       xdt[:, step % 2, g * 512 + left * HD:g * 512 + (h + 1) * HD],
                                       start=True, stop=True)
                    mm.then_inc(intra_ready, 1)
                elif kind == "q":
                    token_major(stage, a[0])
                elif kind == "ga":
                    feature_major(stage, a[0], a[1])
                elif kind in ("z", "zpart"):
                    t, unit = a[0], ("z",) + a[:2]
                    parted = ("zpart",) + a[:2] + (0,) in AT
                    part = (a[2] if kind == "zpart" else Z_PARTS - 1) if parted else 0
                    step = KD // Z_PARTS if parted else KD
                    (w,) = slabs(unit)
                    bank = begin(unit) if part == 0 else bank_of(unit)
                    for k in range(part * step, (part + 1) * step):
                        mm = pe.matmul(bank, hT[:, k, t * P:(t + 1) * P], w[:, k, :], start=(k == 0),
                                       stop=(k == KD - 1))
                    if kind == "z":
                        mm.then_inc(unit_ready, 1)
                elif kind == "score":
                    t, g, i = a
                    n = SCORE[stage]
                    if n == 0:
                        pe.wait_ge(tr_done, len(TR))
                        pe.wait_ge(edges_ready, 2)
                    if n >= 2:
                        pe.wait_ge(prob_ready, n - 1)
                    lhs, tiles = qT[:, i, t * P:(t + 1) * P], local_tiles(t)
                    bank = pair(n)
                    first = 512 - len(tiles) * P
                    if tiles:
                        pe.matmul(bank[:, first:512], lhs, kpad[:, g, tiles[0] * P:(tiles[-1] + 1) * P],
                                  start=True, stop=True)
                        for j, kt in enumerate(tiles):
                            if kt != t:
                                pe.matmul(bank[:, first + j * P:first + (j + 1) * P], identb,
                                          edge_lo if kt < t else edge_hi, start=False, stop=True,
                                          skip_group_check=True)
                    pe.matmul(bank[:, 512:768], lhs, kpad[:, g, SEQ:TOK], start=True, stop=True
                              ).then_inc(score_ready, 1)
                elif kind == "ptr":
                    t, g, i = a
                    n = SCORE[("score",) + a]
                    if n >= 1:
                        pe.wait_ge(pt_done, n)
                    pe.wait_ge(probn_ready, n + 1)
                    nb = len(local_tiles(t)) + NC
                    for j in range(nb):
                        mm = pe.transpose(pt_bank[:, j * P:(j + 1) * P], prob[:, n % 2, (6 - nb + j) * P:(7 - nb + j) * P],
                                          ident)
                    mm.then_inc(pt_ready, 1)
                elif kind == "pv":
                    t, g = a
                    pe.wait_ge(pt_done, SCORE[("score", t, g, A_GROUP - 1)] + 1)
                    tiles = local_tiles(t) + [NX, NX + 1]
                    bank = begin(stage)
                    for j, kt in enumerate(tiles):
                        mm = pe.matmul(bank, vdup[:, kt, g, :, :], probT[:, j, :, :], start=(j == 0),
                                       stop=(j == len(tiles) - 1))
                    mm.then_inc(unit_ready, 1)
                elif kind == "ytr":
                    k, s = a
                    _, first, _, tiles = SEGS[s]
                    pe.wait_ge(y_ready, at("ynorm", first // P + tiles - 1))
                    turn(stage, [yacc[:, first // P + j, k * P:(k + 1) * P] for j in range(tiles)])
                elif kind == "out0":
                    n, t = a
                    if a == (0, 0):
                        wait_done_upto(pe, ("ytr", KD - 1, 1))
                    bank = begin(stage)
                    for k in range(KM):
                        if k % 6 == 0:
                            slab = slab_landing(("out0", n, k // 6))
                        src = gaT[:, k, :] if k < 4 else hT[:, k - 4, :]
                        mm = pe.matmul(bank, src[:, t * P:(t + 1) * P], slab[:, k % 6, :], start=(k == 0),
                                       stop=(k == KM - 1))
                    mm.then_inc(unit_ready, 1)
                elif kind in ("k1", "v1", "q1", "g1"):
                    if stage == ("k1", 0, 0):
                        wait_hT(1)
                    token_major(stage, a[1])
                elif kind == "hq":
                    h = a[0]
                    pe.wait_ge(qk_ready, NT + HEADN[("q1", h // 4, NX - 1)] + 1)
                    turn(stage, [q1v[:, t, h * P:(h + 1) * P] for t in range(NX)])
                elif kind == "hk":
                    h, s = a
                    pe.wait_ge(qk_ready, NT + HEADN[("k1", 1, NT - 1)] + 1)
                    turn(stage, [k1v[:, t, h * P:(h + 1) * P] for t in (range(NX) if s == 0 else range(NX, NT))])
                elif kind == "sc1":
                    h, t, c = a
                    n = SC1[stage]
                    if n == 0:
                        pe.wait_ge(prob_ready, len(SCORE))
                    if n >= 2:
                        pe.wait_ge(prob1_ready, n - 1)
                    if (t, c) == (0, 0):
                        wait_done(pe, ("hq", h))
                        wait_done(pe, ("hk", h, 0))
                        wait_done(pe, ("hk", h, 1))
                    for lo, hi in ((0, 512), (512, TOK)):
                        mm = pe.matmul(pair(n)[:, lo:hi], qpad[:, c, t * P:(t + 1) * P], kT1[:, lo:hi],
                                       start=True, stop=True)
                    mm.then_inc(sc_ready, 1)
                elif kind == "ptr1":
                    n = at(*stage) - 1
                    if n == 0:
                        pe.wait_ge(pt_done, len(SCORE))
                    else:
                        pe.wait_ge(pt1_done, n)
                    pe.wait_ge(a_ready, n + 1)
                    for j in range(NT):
                        mm = pe.transpose(pt_bank[:, j * P:(j + 1) * P], prob1[(n + 1) % 2][:, 0, j * P:(j + 1) * P], ident)
                    mm.then_inc(pt1_ready, 1)
                elif kind == "pv1":
                    h, t = a
                    pe.wait_ge(pt1_done, at(*stage))
                    if stage == ("pv1", 0, 0):
                        wait_done_upto(pe, ("v1", 1, NT - 1))
                    bank = begin(stage)
                    for j in range(NT):
                        mm = pe.matmul(bank[:, 0:P], probT1[:, j, :], v1v[:, j, h * P:(h + 1) * P],
                                       start=(j == 0), stop=(j == NT - 1))
                    mm.then_inc(unit_ready, 1)
                elif kind == "otr":
                    pe.wait_ge(o_ready, a[0] + 1)
                    turn(stage, [g1v[:, t, a[0] * P:(a[0] + 1) * P] for t in range(NX)])
                elif kind == "out1":
                    if a == (0, 0):
                        wait_done_upto(pe, ("otr", C_HEADS - 1))
                    token_major(stage, a[1])

        @block.vector
        def _(dve):
            link = chained(dve, dve_chain)
            V = nc.vector

            def ropes(src, groups, wtab, wrow, token_tile, ta, tb):
                v = src.rearrange("p (h d) -> p h d", d=HD)
                a = ta[:, 0:groups * HD].rearrange("p (h d) -> p h d", d=HD)
                if token_tile >= NX:
                    link(V.tensor_tensor(a, v, wrow.unsqueeze(1).to_broadcast([P, groups, HD]), ALU.mult))
                    return
                cos = wtab[:, 0, token_tile, :].unsqueeze(1).to_broadcast([P, groups, HD])
                V.tensor_tensor(a, v, cos, ALU.mult)
                pairs = src.rearrange("p (m b j) -> p m b j", b=2, j=HD // 4)
                turned = tb[:, 0:groups * HD].rearrange("p (m b j) -> p m b j", b=2, j=HD // 4)
                sin = wtab[:, 1, token_tile, :].rearrange("p (a b j) -> p a b j", b=2, j=HD // 4)
                for b in range(2):
                    for half in range(2):
                        o = turned.rearrange("p (h a) b j -> p h a b j", a=2)[:, :, half, b, :]
                        i = pairs.rearrange("p (h a) b j -> p h a b j", a=2)[:, :, half, 1 - b, :]
                        w = sin[:, half, b, :].unsqueeze(1).to_broadcast([P, groups, HD // 4])
                        last = V.tensor_tensor(o, i, w, ALU.mult)
                link(last)
                link(V.tensor_tensor(ta[:, 0:groups * HD], ta[:, 0:groups * HD], tb[:, 0:groups * HD], ALU.add))

            def gain_tables(tab, raw, wq, wk):
                for w, row in ((0, wq), (1, wk)):
                    V.tensor_tensor(tab[:, w, 0, :, :], raw[:, 0, :, :],
                                    row.unsqueeze(1).to_broadcast([P, NX, HD]), ALU.mult)
                    m = row.rearrange("p (a b j) -> p a b j", a=2, b=2)
                    for half in range(2):
                        for b in range(2):
                            at_ = slice((2 * half + b) * 16, (2 * half + b + 1) * 16)
                            last = V.tensor_tensor(tab[:, w, 1, :, at_], raw[:, 1, :, at_],
                                                   m[:, half, 1 - b, :].unsqueeze(1).to_broadcast([P, NX, 16]),
                                                   ALU.mult)
                link(last)

            V.memset(ones, 1.0)
            V.memset(neg_half, -0.5).then_inc(pool_start, 1)
            dve.wait_ge(const_in, 32)
            V.tensor_copy(identb, ident).then_inc(edges_ready, 1)
            V.tensor_copy(edges[:, P:3 * P], edges_f32).then_inc(edges_ready, 1)

            for stage in STAGES:
                kind, a = stage[0], stage[1:]
                if kind == "params":
                    wait_unit(dve, stage)
                    dst, count = ((vec1, ROWS1), (vec2, ROWS2))[a[0]]
                    V.tensor_copy(dst, bank_of(stage)[:, 0:count]).then_inc(done_sem(stage), 1)
                    wait_done(dve, stage)
                    if a[0] == 0:
                        dve.wait_ge(tanh_c, 1)
                        link(V.scalar_tensor_tensor(out=silu_c, in0=silu_c, scalar=1.0, in1=vec1[:, 0:16],
                                                    op0=ALU.add, op1=ALU.mult))
                        V.tensor_scalar(silu_c, silu_c, 0.5, None, ALU.mult).then_inc(silu_c_ready, 1)
                    else:
                        link(V.tensor_scalar(halftap, vec2[:, 0:ROW_SSM], 0.5, None, ALU.mult))
                        link(V.tensor_scalar(head_gain, vec2[:, ROW_HEAD:ROW_HEAD + 1],
                                             0.5 * (1.0 - LAMBDA_INIT), None, ALU.mult))
                        dve.wait_ge(bc_in, 16 * 8)
                        link(V.tensor_scalar(nsink, sink, -1.0, None, ALU.mult))
                elif kind == "modcol":
                    layer = a[0]
                    wait_unit(dve, stage)
                    cols = mod_cols.rearrange("p (r n) -> p r n", r=2)
                    V.tensor_tensor(cols, bank_of(stage)[:, 0:32].rearrange(
                                        "p (n r) -> p r n" if layer == 0 else "p (r n) -> p r n", r=2),
                                    vec1[:, ROW_MODB + 16 * layer:ROW_MODB + 16 * (layer + 1)].unsqueeze(1)
                                    .to_broadcast([P, 2, 16]), ALU.add).then_inc(done_sem(stage), 1)
                    wait_done(dve, stage)
                    gains = gain_cols.rearrange("p (r n) -> p r n", r=2)
                    V.scalar_tensor_tensor(
                        out=gains, in0=cols[:, :, 8:16], scalar=1.0,
                        in1=vec1[:, ROW_NORM + 8 * layer:ROW_NORM + 8 * (layer + 1)].unsqueeze(1)
                        .to_broadcast([P, 2, 8]), op0=ALU.add, op1=ALU.mult).then_inc(cols_ready, 1)
                elif kind == "norm":
                    layer, t = a
                    dve.wait_ge(rstd_ready, at(*stage))
                    V.tensor_scalar(xhat[:, t, :], xin[:, t, :], rs_x[:, layer * NT + t:layer * NT + t + 1], None,
                                    ALU.mult).then_inc(xhat_ready, 1)
                elif kind == "trn":
                    layer, k, s = a
                    n = TRN[stage]
                    if n % 2 == 0:
                        _, first, count, _ = SEGS[s]
                        dve.wait_ge(cols_ready, at("modcol", layer))
                        dve.wait_ge(trn_ready, n + 1)
                        bank = ps[:, 2 + n % 4, :]
                        for i in range(k, k + 1 + s):
                            last = V.tensor_scalar(
                                hT[:, i, first:first + count], bank[:, (i - k) * count:(i - k + 1) * count],
                                gain_cols[:, 8 * s + i:8 * s + i + 1], mod_cols[:, 16 * s + i:16 * s + i + 1],
                                ALU.mult, ALU.add)
                        last.then_inc(trn_done[0], 1)
                elif kind == "xbc":
                    f, s = a
                    _, first, count, _ = SEGS[s]
                    wait_unit(dve, stage)
                    src = bank_of(stage)
                    dst = conv[:, (at("xbc", f, 0) // 2) % 3, first:first + count]
                    tap = lambda j: halftap[:, j * FT + f:j * FT + f + 1]
                    link(V.tensor_scalar(dst, src[:, 0:count], tap(2), halftap[:, ROW_CONVB + f:ROW_CONVB + f + 1],
                                         ALU.mult, ALU.add))
                    for j in (0, 1, 3, 4):
                        lo, hi = max(0, 2 - j), min(count, count + 2 - j)
                        ins_ = V.scalar_tensor_tensor(out=dst[:, lo:hi], in0=src[:, lo + j - 2:hi + j - 2],
                                                      scalar=tap(j), in1=dst[:, lo:hi], op0=ALU.mult, op1=ALU.add)
                        if j < 4:
                            link(ins_)
                        else:
                            ins_.then_inc(done_sem(stage), 1)
                elif kind == "silu":
                    f = a[0]
                    n = at(*stage) - 1
                    dve.wait_ge(conv_tanh, n + 1)
                    wait_done_upto(dve, ("xbc", f, 1))
                    src = conv[:, (at("xbc", f, 0) // 2) % 3, :]
                    if f >= 8:
                        dst = bct[:, f - 8, :]
                    else:
                        dst = xsT[:, f % 2, :]
                        if f >= 2:
                            dve.wait_ge(tr_ready, TR[("xtr", f - 2)] + 1)
                    V.scalar_tensor_tensor(out=dst, in0=conv_th[:, n % 2, :], scalar=1.0, in1=src,
                                           op0=ALU.add, op1=ALU.mult).then_inc(silu_ready, 1)
                elif kind == "dtv":
                    if True:
                        wait_done_upto(dve, ("kvdt", NT - 1))
                        raw4 = dt_raw.rearrange("p (t d h) -> p d t h", t=NT, d=2)
                        v, e, u, w, m, n_ = (dt_tmp[:, j, :] for j in range(6))
                        v4 = v.rearrange("p (d t h) -> p d t h", d=2, t=NT)
                        for d in range(2):
                            last = V.tensor_tensor(v4[:, d, :, :], raw4[:, d, :, :],
                                                   dtb[:, d * 16:(d + 1) * 16].unsqueeze(1)
                                                   .to_broadcast([P, NT, 16]), ALU.add)
                        link(last)
                        link(V.tensor_scalar(m, v, -1.0, None, ALU.mult))
                        V.tensor_tensor(n_, v, m, ALU.min).then_inc(dt_dve, 1)
                        dve.wait_ge(dt_exp, 1)
                        link(V.tensor_scalar(u, e, 1.0, None, ALU.add))
                        link(V.tensor_scalar(w, u, 1.0, 2.0 ** -24, ALU.subtract, ALU.max))
                        V.tensor_scalar(m, u, 0.0, None, ALU.add).then_inc(dt_dve, 1)
                        link(V.reciprocal(w, w))
                        link(V.tensor_tensor(w, w, e, ALU.mult))
                        dve.wait_ge(dt_exp, 2)
                        link(V.tensor_tensor(w, w, m, ALU.mult))
                        link(V.scalar_tensor_tensor(out=dt_v, in0=v, scalar=0.0, in1=w, op0=ALU.max, op1=ALU.add))
                        dve.wait_ge(dt_exp, 3)
                        link(V.tensor_scalar(alog, alog, -1.0, None, ALU.mult))
                        for d in range(2):
                            last = V.tensor_tensor(
                                dta_v[:, d * 96:(d + 1) * 96].rearrange("p (t h) -> p t h", t=NT),
                                dt_v[:, d * 96:(d + 1) * 96].rearrange("p (t h) -> p t h", t=NT),
                                alog[:, d * 16:(d + 1) * 16].unsqueeze(1).to_broadcast([P, NT, 16]), ALU.mult)
                            if d == 0:
                                link(last)
                        last.then_inc(dta_ready, 1)
                elif kind == "cb":
                    d, c = a
                    n = SEGU[stage]
                    dve.wait_ge(seg_ready, n + 1)
                    r = STEP[a] % 2
                    V.tensor_tensor(cbm[:, r, :, :], ps[:, 2 + n % 2, 0:2 * P].rearrange("p (g t) -> p g t", g=2),
                                    (le, ge)[d].unsqueeze(1).to_broadcast([P, 2, P]), ALU.mult
                                    ).then_inc(seg_done[n % 2], 1)
                    dve.wait_ge(seg_done[n % 2], n // 2 + 1)
                elif kind == "seg":
                    d, c, q = a
                    n, u = SEG[stage], SEGU[stage]
                    dve.wait_ge(seg_done[u % 2], u // 2 + 1)
                    e = emat[:, n % 3, :].rearrange("p (h t) -> p h t", h=4)
                    V.tensor_tensor(e, e, cbm[:, STEP[(d, c)] % 2, q // 2, :].unsqueeze(1).to_broadcast([P, 4, P]),
                                    ALU.mult).then_inc(emat_ready, 1)
                elif kind == "inter":
                    d, c = a
                    if stage + (0,) in STATEU:
                        for g in range(B_G):
                            n = STATEU[stage + (g,)]
                            dve.wait_ge(st_ready, n + 1)
                            ela = decay[:, 2 * d * 96 + c * 16 + g * 8:2 * d * 96 + c * 16 + g * 8 + 8]
                            V.tensor_tensor(y_in[:, g, :].rearrange("p (h d) -> p h d", h=8),
                                            ps[:, (4, 7)[n % 2], :].rearrange("p (h d) -> p h d", h=8),
                                            ela.unsqueeze(2).to_broadcast([P, 8, HD]), ALU.mult).then_inc(st_done, 1)
                        dve.wait_ge(st_done, n + 1)
                elif kind == "state":
                    d, c = a
                    if stage + (0,) in STATEU:
                        first = a in FIRST_STEP
                        if not first:
                            cd = cdec[:, d * 96 + c * 16:d * 96 + c * 16 + 16]
                            h3 = hst.rearrange("p (h d) -> p h d", h=16)
                            link(V.tensor_tensor(h3, h3, cd.unsqueeze(2).to_broadcast([P, 16, HD]), ALU.mult))
                        for g in range(B_G):
                            n = STATEU[stage + (g,)]
                            dve.wait_ge(st_ready, n + 1)
                            part, src = hst[:, g * 512:(g + 1) * 512], ps[:, (4, 7)[n % 2], :]
                            if first:
                                V.tensor_copy(part, src).then_inc(st_done, 1)
                            else:
                                V.tensor_tensor(part, part, src, ALU.add).then_inc(st_done, 1)
                        dve.wait_ge(st_done, n + 1)
                        V.tensor_copy(stat[:, 186:187], ones[:, 0:1]).then_inc(h_ready, 1)
                elif kind == "ysum":
                    d, c, g = a
                    step = STEP[(d, c)]
                    dve.wait_ge(intra_ready, SEG[("seg", d, c, 2 * g)] + 1)
                    part = yacc[:, c, g * 512:(g + 1) * 512]
                    if (d, c) in FIRST_STEP:
                        dve.wait_ge(xdt_ready, step + 1)
                        V.tensor_tensor(part, part, ps[:, 5 + g, :], ALU.add).then_inc(intra_done, 1)
                    else:
                        V.tensor_tensor(y_in[:, g, :], y_in[:, g, :], ps[:, 5 + g, :], ALU.add
                                        ).then_inc(intra_done, 1)
                        dve.wait_ge(intra_done, 2 * step + g + 1)
                        dve.wait_ge(xdt_ready, step + 1)
                        link(V.tensor_tensor(part, part, y_in[:, g, :], ALU.add))
                elif kind == "ga":
                    f, s = a
                    _, first, count, _ = SEGS[s]
                    n = GATE[stage]
                    dve.wait_ge(gate_tanh, n + 1)
                    V.scalar_tensor_tensor(out=gaT[:, f, first:first + count], in0=gate_th[:, 0:count],
                                           scalar=1.0, in1=bank_of(stage)[:, 0:count], op0=ALU.add, op1=ALU.mult
                                           ).then_inc(done_sem(stage), 1)
                elif kind in ("q", "k1", "q1"):
                    n = HEADU[stage]
                    groups = 10 if kind == "q" else 8
                    t = a[-1]
                    if n == 0:
                        dve.wait_ge(rope_in, 16)
                        gain_tables(rope_t, rope_raw, qkw[:, 0:64], qkw[:, 64:128])
                        V.memset(kpad[HD:P, 0, :], 0.0)
                        V.memset(kpad[0:HD, 1, :], 0.0).then_inc(pads_ready, 1)
                    if stage == ("k1", 0, 0):
                        dve.wait_ge(rope1_in, 16)
                        dve.wait_ge(x1_ready, 2 * NT)
                        gain_tables(rope_t1, rope_raw1, qkw[:, 128:192], qkw[:, 192:256])
                        V.memset(qpad[HD:P, 0, :], 0.0)
                        V.memset(qpad[0:HD, 1, :], 0.0).then_inc(pads_ready, 1)
                        dve.wait_ge(lam_in, 16)
                        l4 = lam_p.rearrange("p (a b d) -> p a b d", a=2, b=2)
                        link(V.tensor_tensor(l4[:, :, 0, :], l4[:, :, 0, :], l4[:, :, 1, :], ALU.mult))
                        V.tensor_reduce(lam_e[:, 0:2], l4[:, :, 0, :], AXX, ALU.add).then_inc(lam_ready, 1)
                    sq = (qk_sq if kind == "q" else sq1)[:, 0:groups * HD]
                    if n >= 1:
                        dve.wait_ge(qk_ready, n)
                    dve.wait_ge(head_sq, n + 1)
                    V.tensor_reduce(ss_h[:, 0:groups], sq.rearrange("p (h d) -> p h d", d=HD), AXX, ALU.add
                                    ).then_inc(head_ss, 1)
                    if kind == "q":
                        buf, ta = qk[:, t % 2, :], rope_a
                        ropes(buf[:, 0:A_W], 8, rope_t[:, 0], qkw[:, 0:64], t, rope_a, rope_b)
                        ropes(buf[:, A_W:640], 2, rope_t[:, 1], qkw[:, 64:128], t, rope_a[:, A_W:640],
                              rope_b[:, A_W:640])
                    else:
                        buf = (k1v if kind == "k1" else q1v)[:, t, a[0] * SLAB:(a[0] + 1) * SLAB]
                        w = 1 if kind == "k1" else 0
                        ta = rope_a1
                        ropes(buf, 8, rope_t1[:, w], qkw[:, 128 + 64 * w:192 + 64 * w], t, rope_a1, rope_b1)
                    dve.wait_ge(head_rstd, n + 1)
                    if kind == "q":
                        for g in range(A_KV):
                            V.tensor_tensor(
                                buf[:, 0:A_W].rearrange("p (i g d) -> p g i d", g=A_KV, d=HD)[:, g, :, :],
                                ta[:, g * 256:(g + 1) * 256].rearrange("p (i d) -> p i d", d=HD),
                                rs_h[:, 4 * g:4 * g + 4].unsqueeze(2).to_broadcast([P, A_GROUP, HD]), ALU.mult)
                        buf, ta, first, groups = buf[:, A_W:640], ta[:, A_W:640], 8, 2
                    else:
                        first = 0
                    V.tensor_tensor(buf.rearrange("p (h d) -> p h d", d=HD),
                                    ta[:, 0:groups * HD].rearrange("p (h d) -> p h d", d=HD),
                                    rs_h[:, first:first + groups].unsqueeze(2).to_broadcast([P, groups, HD]), ALU.mult
                                    ).then_inc(qk_ready, 1)
                elif kind in ("score", "sc1"):
                    if kind == "score":
                        t, g, i = a
                        n = SCORE[stage]
                        dve.wait_ge(score_ready, n + 1)
                        first = 512 - len(local_tiles(t)) * P
                        r = n % 8
                        link(V.tensor_reduce(rmax[:, r:r + 1], pair(n)[:, first:768], AXX, ALU.max))
                        h = 4 * g + i
                        V.tensor_scalar(nmax[:, r:r + 1], rmax[:, r:r + 1], -SCALE, nsink[:, h:h + 1],
                                        ALU.mult, ALU.min).then_inc(nmax_ready, 1)
                    else:
                        n = SC1[stage]
                        dve.wait_ge(sc_ready, n + 1)
                        r = n % 8
                        link(V.tensor_reduce(rmax[:, r:r + 1], pair(n)[:, 0:TOK], AXX, ALU.max))
                        V.tensor_scalar(nmax[:, r:r + 1], rmax[:, r:r + 1], -SCALE, None, ALU.mult
                                        ).then_inc(nmax1, 1)
                elif kind == "pnorm":
                    t, g, i = a
                    n = SCORE[("score",) + a]
                    r, first = n % 8, 512 - len(local_tiles(t)) * P
                    dve.wait_ge(prob_ready, n + 1)
                    link(V.tensor_scalar(rinv[:, r:r + 1], rsum[:, r:r + 1], esink[:, r:r + 1], 2.0, ALU.add, ALU.mult))
                    link(V.reciprocal(rinv[:, r:r + 1], rinv[:, r:r + 1]))
                    V.tensor_scalar(prob[:, n % 2, first:768], prob[:, n % 2, first:768], rinv[:, r:r + 1], None,
                                    ALU.mult).then_inc(probn_ready, 1)
                elif kind == "pv":
                    t, g = a
                    wait_unit(dve, stage)
                    src = bank_of(stage).rearrange("p (j u t) -> p u j t", u=2, t=P)
                    for half in range(2):
                        rows = slice(half * HD, (half + 1) * HD)
                        dst = gaT[rows, 2 * g:2 * g + 2, t * P:(t + 1) * P]
                        last = V.tensor_tensor(dst, src[rows, half, :, :], dst, ALU.mult)
                    last.then_inc(done_sem(stage), 1)
                elif kind == "z":
                    t, n_ = a
                    n = GATE[stage]
                    dve.wait_ge(gate_tanh, n + 1)
                    V.scalar_tensor_tensor(out=zg, in0=gate_thz[:, n % 2, :], scalar=1.0, in1=bank_of(stage),
                                           op0=ALU.add, op1=ALU.mult).then_inc(done_sem(stage), 1)
                    wait_done(dve, stage)
                    part = yacc[:, t, n_ * SLAB:(n_ + 1) * SLAB]
                    V.tensor_tensor(part, part, zg, ALU.mult).then_inc(gated_y, 1)
                elif kind == "ynorm":
                    t = a[0]
                    dve.wait_ge(y_rstd, t + 1)
                    V.tensor_scalar(yacc[:, t, :], yacc[:, t, :], rs_y[:, t:t + 1], 0.5, ALU.mult, ALU.mult
                                    ).then_inc(y_ready, 1)
                elif kind == "ytr":
                    k, s = a
                    if s == 0:
                        wait_unit(dve, stage)
                        V.tensor_scalar(hT[:, k, 0:SEQ], bank_of(stage), vec2[:, ROW_SSM + k:ROW_SSM + k + 1], None,
                                        ALU.mult).then_inc(done_sem(stage), 1)
                elif kind == "gatesum":
                    layer = a[0]
                    if layer == 0:
                        dve.wait_ge(gate_in, 16 * 3)
                        link(V.tensor_tensor(gate_bc, gate_bc, gate_b.unsqueeze(1).to_broadcast([P, 2, D]), ALU.add))
                    else:
                        dve.wait_ge(gate1_in, 16 * 2)
                        link(V.tensor_tensor(gate_bc1, gate_bc1, gate_b1, ALU.add))
                elif kind in ("out0", "out1"):
                    n, t = a
                    u = at(*stage) - 1
                    if stage == ("out0", 0, 0):
                        dve.wait_ge(xres_in, 16 * NT)
                    wait_unit(dve, stage)
                    if kind == "out0":
                        tmp, gate = res_tmp[:, u % 2, :], gate_bc[:, 0 if t < NX else 1, n * SLAB:(n + 1) * SLAB]
                    else:
                        tmp, gate = res_tmp1[:, u % 2, :], gate_bc1[:, n * SLAB:(n + 1) * SLAB]
                    if u >= 2:
                        dve.wait_ge(x1_ready if kind == "out0" else out_ready, u - 1)
                    V.tensor_tensor(tmp, bank_of(stage), gate, ALU.mult).then_inc(done_sem(stage), 1)
                    wait_done(dve, stage)
                    part = x1[:, t, n * SLAB:(n + 1) * SLAB]
                    V.tensor_tensor(part, part, tmp, ALU.add).then_inc(x1_ready if kind == "out0" else out_ready, 1)
                elif kind == "g1":
                    n_, t = a
                    n = GATE[stage]
                    dve.wait_ge(gate_tanh, n + 1)
                    V.scalar_tensor_tensor(out=g1v[:, t, n_ * SLAB:(n_ + 1) * SLAB], in0=gate_th1, scalar=1.0,
                                           in1=bank_of(stage), op0=ALU.add, op1=ALU.mult
                                           ).then_inc(done_sem(stage), 1)
                elif kind == "comb1":
                    h, t = a
                    n = at(*stage) - 1
                    if n == 0:
                        dve.wait_ge(lam_exp, 1)
                        link(V.tensor_tensor(neg_lam, lam_e[:, 3:4], lam_e[:, 2:3], ALU.subtract))
                        link(V.tensor_scalar(neg_lam, neg_lam, -LAMBDA_INIT, None, ALU.add))
                    dve.wait_ge(prob1_ready, 2 * n + 2)
                    r = (2 * n) % 8
                    link(V.reciprocal(rinv[:, r:r + 2], rsum[:, r:r + 2]))
                    link(V.scalar_tensor_tensor(out=rinv[:, r + 1:r + 2], in0=rinv[:, r + 1:r + 2], scalar=neg_lam,
                                                in1=rsum[:, r:r + 1], op0=ALU.mult, op1=ALU.mult))
                    p0, p1 = (prob1[(n + 1) % 2][:, c, :] for c in range(2))
                    V.scalar_tensor_tensor(out=p0, in0=p1, scalar=rinv[:, r + 1:r + 2], in1=p0,
                                           op0=ALU.mult, op1=ALU.add).then_inc(a_ready, 1)
                elif kind == "pv1":
                    h, t = a
                    dve.wait_ge(o_sq, at(*stage))
                    if h % 4 == 0:
                        wait_done(dve, ("g1", h // 4, t))
                    part = g1v[:, t, h * P:(h + 1) * P]
                    r = 2 * (at(*stage) - 1) % 8
                    V.scalar_tensor_tensor(out=part, in0=bank_of(stage)[:, 0:P], scalar=rinv[:, r:r + 1], in1=part,
                                           op0=ALU.mult, op1=ALU.mult).then_inc(done_sem(stage), 1)
                elif kind == "hnorm":
                    h = a[0]
                    dve.wait_ge(o_rstd, h + 1)
                    for tile in range(NX):
                        wait_done(dve, ("pv1", h, tile))
                    g3 = g1v[:, :, h * P:(h + 1) * P]
                    V.tensor_tensor(g3, g3, rs_o[:, h * NX:(h + 1) * NX].unsqueeze(2).to_broadcast([P, NX, P]),
                                    ALU.mult).then_inc(o_ready, 1)
                elif kind == "otr":
                    h = a[0]
                    if h % 2 == 0:
                        wait_unit(dve, stage)
                        V.tensor_scalar(hT[:, h, 0:SEQ], bank_of(stage), head_gain, None, ALU.mult
                                        ).then_inc(done_sem(stage), 1)

        @block.scalar
        def _(act):
            link = chained(act, act_chain)
            A = nc.scalar
            act.dma_start(slab_ap(SLABS[0]), slab_source(SLABS[0])).then_inc(slab_in[0], 16)
            for stage in STAGES:
                kind, a = stage[0], stage[1:]
                if kind == "params" and a[0] == 0:
                    wait_done(act, stage)
                    A.activation(silu_c, vec1[:, 0:16], ACT.Tanh, scale=0.5).then_inc(tanh_c, 1)
                elif kind == "mod":
                    layer, s = a
                    wait_unit(act, stage)
                    if (layer, s) in MOD_ON_CHIP:
                        A.copy(mod_rows0[:, s * SLAB:(s + 1) * SLAB], bank_of(stage)[0:2, :]
                               ).then_inc(done_sem(stage), 1)
                        continue
                    if MOD_STORE[stage] >= 1:
                        act.wait_ge(mod_stored, 16 * MOD_STORE[stage])
                    A.copy(mod_row[0:2, :], bank_of(stage)[0:2, :]).then_inc(done_sem(stage), 1)
                    wait_done(act, stage)
                    act.dma_start(mod_dram[layer, :, s * SLAB:(s + 1) * SLAB], mod_row[0:2, :]
                                  ).then_inc(mod_stored, 16)
                elif kind == "modin":
                    act.wait_ge(mod_stored, 16 * len(MOD_STORE))
                    act.dma_start(mod_blk, mod_dram[1, :, 0:2 * D].rearrange("r (k p) -> r k p", p=P)
                                  ).then_inc(mod_rows, 16)
                elif kind == "norm":
                    layer, t = a
                    if layer == 0:
                        act.wait_ge(x_in_s[t], 16)
                    else:
                        act.wait_ge(x1_ready, at("out0", 1, t))
                    if at(*stage) > 1:
                        act.wait_ge(sq_ready, at(*stage) - 1)
                    n = layer * NT + t
                    A.activation(junk if layer == 0 else junk1, xin[:, t, :], ACT.Square, accum_out=ss_x[:, n:n + 1]
                                 ).then_inc(sq_ready, 1)
                elif kind == "trn":
                    layer, k, s = a
                    n = TRN[stage]
                    if n % 2 == 1:
                        _, first, count, _ = SEGS[s]
                        act.wait_ge(cols_ready, at("modcol", layer))
                        act.wait_ge(trn_ready, n + 1)
                        bank = ps[:, 2 + n % 4, :]
                        for i in range(k, k + 1 + s):
                            last = A.activation(hT[:, i, first:first + count],
                                                bank[:, (i - k) * count:(i - k + 1) * count], ACT.Identity,
                                                scale=gain_cols[:, 8 * s + i:8 * s + i + 1],
                                                bias=mod_cols[:, 16 * s + i:16 * s + i + 1])
                        last.then_inc(trn_done[1], 1)
                elif kind == "silu":
                    f = a[0]
                    n = at(*stage) - 1
                    wait_done_upto(act, ("xbc", f, 1))
                    if n >= 2:
                        act.wait_ge(silu_ready, n - 1)
                    A.activation(conv_th[:, n % 2, :], conv[:, (at("xbc", f, 0) // 2) % 3, :], ACT.Tanh
                                 ).then_inc(conv_tanh, 1)
                elif kind == "xtr":
                    f = a[0]
                    act.wait_ge(tr_ready, TR[stage] + 1)
                    src = pair(TR[stage])[:, 0:TOK].rearrange("p (t n) -> p t n", t=NT)
                    dst = btok[:, :, f - 8, :] if f >= 8 else xs[:, :, f * P:(f + 1) * P]
                    A.copy(dst, src).then_inc(tr_done, 1)
                elif kind == "kvdt":
                    t = a[0]
                    wait_unit(act, stage)
                    bank = bank_of(stage)
                    A.copy(kraw[:, t, :], bank[:, 0:P])
                    A.copy(vdup[:, t, :, :, :], bank[:, P:2 * P].rearrange("p (g d) -> p g d", g=2).unsqueeze(2)
                           .to_broadcast([P, 2, 2, HD]))
                    A.copy(dt_raw[:, t * 32:(t + 1) * 32], bank[:, 2 * P:KVDT]).then_inc(done_sem(stage), 1)
                elif kind == "dtv":
                    v, e, u, w, m, n_ = (dt_tmp[:, j, :] for j in range(6))
                    act.wait_ge(dt_dve, 1)
                    A.activation(e, n_, ACT.Exp).then_inc(dt_exp, 1)
                    act.wait_ge(dt_dve, 2)
                    A.activation(m, m, ACT.Ln).then_inc(dt_exp, 1)
                    A.activation(alog, alog, ACT.Exp).then_inc(dt_exp, 1)
                elif kind == "dt":
                    if a[0] == 0:
                        wait_unit(act, stage)
                        A.activation(decay, bank_of(stage)[:, 0:384], ACT.Exp).then_inc(done_sem(stage), 1)
                    else:
                        wait_unit(act, stage)
                        A.activation(cdec, bank_of(stage)[:, 0:192], ACT.Exp).then_inc(done_sem(stage), 1)
                elif kind == "seg":
                    n, u = SEG[stage], SEGU[stage]
                    act.wait_ge(seg_ready, u + 1)
                    if n >= 3:
                        act.wait_ge(intra_ready, n - 2)
                    A.activation(emat[:, n % 3, :], ps[:, 2 + u % 2, :], ACT.Exp).then_inc(seg_done[u % 2], 1)
                elif kind in ("ga", "z", "g1"):
                    n = GATE[stage]
                    count = SEGS[a[1]][2] if kind == "ga" else SLAB
                    wait_unit(act, stage)
                    dst = {"ga": gate_th[:, 0:count], "z": gate_thz[:, n % 2, :], "g1": gate_th1}[kind]
                    back = 2 if kind == "z" else 1
                    if n >= back:
                        wait_done_upto(act, GATES[n - back])
                    if n == 0:
                        act.wait_ge(silu_ready, at("silu", 7))
                    A.activation(dst, bank_of(stage)[:, 0:count], ACT.Tanh, scale=0.5).then_inc(gate_tanh, 1)
                elif kind in ("q", "k1", "q1"):
                    n = HEADU[stage]
                    t = a[-1]
                    wait_unit(act, stage)
                    if kind == "q":
                        if t >= 2:
                            act.wait_ge(tr_ready, TR[("qtr", t - 2)] + 1)
                        buf, sq = qk[:, t % 2, :], qk_sq
                        link(A.copy(buf[:, A_W:640], kraw[:, t, :]))
                        A.copy(buf[:, 0:A_W], bank_of(stage)).then_inc(done_sem(stage), 1)
                    else:
                        buf, sq = (k1v if kind == "k1" else q1v)[:, t, a[0] * SLAB:(a[0] + 1) * SLAB], sq1
                        if stage == ("k1", 0, 0):
                            act.wait_ge(pads_ready, 2)
                        A.copy(buf, bank_of(stage)).then_inc(done_sem(stage), 1)
                    wait_done(act, stage)
                    if n >= 1:
                        act.wait_ge(head_ss, n)
                    A.activation(sq, buf, ACT.Square).then_inc(head_sq, 1)
                elif kind == "qtr":
                    t = a[0]
                    if t == 0:
                        act.wait_ge(pads_ready, 1)
                    act.wait_ge(tr_ready, TR[stage] + 1)
                    src = pair(TR[stage])
                    at_ = slice(t * P, (t + 1) * P)
                    A.copy(qT[:, :, at_], src[:, 0:512].rearrange("p (i t) -> p i t", i=4))
                    A.copy(kpad[0:HD, 0, at_], src[0:HD, 512:640])
                    A.copy(kpad[HD:P, 1, at_], src[HD:P, 512:640]).then_inc(tr_done, 1)
                elif kind == "expo":
                    t, g, i = a
                    n = SCORE[("score",) + a]
                    r, h, first = n % 8, 4 * g + i, 512 - len(local_tiles(t)) * P
                    act.wait_ge(nmax_ready, n + 1)
                    A.activation(esink[:, r:r + 1], sink[:, h:h + 1], ACT.Exp, bias=nmax[:, r:r + 1])
                    A.activation(prob[:, n % 2, first:768], pair(n)[:, first:768], ACT.Exp, bias=nmax[:, r:r + 1],
                                 scale=SCALE, accum_out=rsum[:, r:r + 1]).then_inc(prob_ready, 1)
                elif kind == "ptr":
                    t, g, i = a
                    n = SCORE[("score",) + a]
                    act.wait_ge(pt_ready, n + 1)
                    nb = len(local_tiles(t)) + NC
                    group = at("pv", t, g)
                    if i == 0 and group > 1:
                        wait_unit(act, PVS[group - 2])
                    A.copy(probT[:, 0:nb, i, :], pt_bank[:, 0:nb * P].rearrange("p (b t) -> p b t", b=nb)
                           ).then_inc(pt_done, 1)
                elif kind == "ysq":
                    t = a[0]
                    act.wait_ge(gated_y, 2 * NT)
                    if t >= 1:
                        act.wait_ge(y_sq, t)
                    A.activation(y_junk, yacc[:, t, :], ACT.Square, scale=0.5, accum_out=ss_y[:, t:t + 1]
                                 ).then_inc(y_sq, 1)
                elif kind == "ytr":
                    k, s = a
                    if s == 1:
                        wait_unit(act, stage)
                        A.activation(hT[:, k, SEQ:TOK], bank_of(stage)[:, 0:CTX], ACT.Copy,
                                     scale=vec2[:, ROW_SSM + k:ROW_SSM + k + 1]).then_inc(done_sem(stage), 1)
                elif kind == "xres":
                    act.wait_ge(xdt_ready, len(STEPS))
                    act.wait_ge(xw_ready, len(STEPS) - 2)
                    for t in range(NT):
                        src = x_in[t * P:(t + 1) * P, :] if t < NX else ctx_in[(t - NX) * P:(t - NX + 1) * P, :]
                        act.dma_start(xin[:, t, :], src).then_inc(xres_in, 16)
                elif kind == "gates":
                    layer = a[0]
                    act.wait_ge(mod_stored, 16 * len(MOD_STORE))
                    if layer == 0:
                        act.wait_ge(st_done, len(STATEU))
                        act.wait_ge(seg_done[0], len([s for s in SEGU.values() if s % 2 == 0]))
                        act.wait_ge(seg_done[1], len([s for s in SEGU.values() if s % 2 == 1]))
                        act.dma_start(rope_raw.rearrange("p a t d -> p (a t d)"), ins["rope"]).then_inc(rope_in, 16)
                        for r in range(2):
                            act.dma_start(gate_bc[:, r, :], mod_dram[0, r, 2 * D:3 * D].partition_broadcast(P)
                                          ).then_inc(gate_in, 16)
                        act.dma_start(gate_b, ins["mod_b"][0, 2 * D:3 * D].partition_broadcast(P)
                                      ).then_inc(gate_in, 16)
                    else:
                        wait_unit(act, ("hk", C_HEADS - 1, 0))
                        act.dma_start(gate_bc1, mod_dram[1, 0, 2 * D:3 * D].partition_broadcast(P)
                                      ).then_inc(gate1_in, 16)
                        act.dma_start(gate_b1, ins["mod_b"][1, 2 * D:3 * D].partition_broadcast(P)
                                      ).then_inc(gate1_in, 16)
                elif kind in ("hq", "hk"):
                    h = a[0]
                    wait_unit(act, stage)
                    bank = bank_of(stage)
                    if kind == "hq":
                        if h == 0:
                            act.wait_ge(pads_ready, 2)
                        else:
                            act.wait_ge(sc_ready, SC1[("sc1", h - 1, NX - 1, 1)] + 1)
                        A.copy(qpad[0:HD, 0, :], bank[0:HD, :])
                        A.copy(qpad[HD:P, 1, :], bank[HD:P, :]).then_inc(done_sem(stage), 1)
                    else:
                        lo, hi = ((0, SEQ), (SEQ, TOK))[a[1]]
                        A.copy(kT1[:, lo:hi], bank[:, 0:hi - lo]).then_inc(done_sem(stage), 1)
                elif kind == "v1":
                    if a == (0, 0):
                        act.wait_ge(lam_ready, 1)
                        A.activation(lam_e[:, 2:4], lam_e[:, 0:2], ACT.Exp).then_inc(lam_exp, 1)
                    wait_unit(act, stage)
                    A.copy(v1v[:, a[1], a[0] * SLAB:(a[0] + 1) * SLAB], bank_of(stage)).then_inc(done_sem(stage), 1)
                elif kind == "exp1":
                    h, t = a
                    place = prob1[at(*stage) % 2]
                    for c in range(2):
                        n = SC1[("sc1", h, t, c)]
                        r = n % 8
                        act.wait_ge(nmax1, n + 1)
                        if n < 4:
                            act.wait_ge(qk_ready, len(HEADU))
                        else:
                            act.wait_ge(pt1_ready, n // 2 - 1)
                        A.activation(place[:, c, :], pair(n)[:, 0:TOK], ACT.Exp, bias=nmax[:, r:r + 1],
                                     scale=SCALE, accum_out=rsum[:, r:r + 1]).then_inc(prob1_ready, 1)
                elif kind == "ptr1":
                    n = at(*stage) - 1
                    act.wait_ge(pt1_ready, n + 1)
                    if n >= 1:
                        wait_unit(act, PV1S[n - 1])
                    A.copy(probT1, pt_bank[:, 0:TOK].rearrange("p (b t) -> p b t", b=NT)).then_inc(pt1_done, 1)
                elif kind == "pv1":
                    h, t = a
                    wait_unit(act, stage)
                    if at(*stage) > 1:
                        act.wait_ge(o_sq, at(*stage) - 1)
                    r = 2 * (at(*stage) - 1) % 8
                    A.activation(le, bank_of(stage)[:, 0:P], ACT.Square, scale=rinv[:, r:r + 1],
                                 accum_out=ss_o[:, h * NX + t:h * NX + t + 1]).then_inc(o_sq, 1)
                elif kind == "otr":
                    h = a[0]
                    if h % 2 == 1:
                        wait_unit(act, stage)
                        A.activation(hT[:, h, 0:SEQ], bank_of(stage), ACT.Copy, scale=head_gain
                                     ).then_inc(done_sem(stage), 1)
                if stage == ("norm", 1, NT - 1):
                    act.dma_start(rope_raw1.rearrange("p a t d -> p (a t d)"), ins["rope"]).then_inc(rope1_in, 16)
                    act.dma_start(lam_p, ins["od_lambda"][0].rearrange("a d -> (a d)").partition_broadcast(P)
                                  ).then_inc(lam_in, 16)

        @block.gpsimd
        def _(pool):
            link = chained(pool, pool_chain)
            G = nc.gpsimd
            for dst, src in ((qkw[:, 0:64], ins["ev_q_norm"][0]), (qkw[:, 64:128], ins["ev_k_norm"][0]),
                             (qkw[:, 128:192], ins["od_q_norm"][0]), (qkw[:, 192:256], ins["od_k_norm"][0]),
                             (sink, ins["ev_sink"][0]), (dtb, ins["ev_dt_bias"][0].rearrange("a h -> (a h)")),
                             (alog, ins["ev_a_log"][0].rearrange("a h -> (a h)")), (dskip, ins["ev_d_skip"][0])):
                pool.dma_start(dst, src.partition_broadcast(P)).then_inc(bc_in, 16)
            pool.wait_ge(slab_in[1], 16)
            for t in range(NT):
                src = x_in[t * P:(t + 1) * P, :] if t < NX else ctx_in[(t - NX) * P:(t - NX + 1) * P, :]
                pool.dma_start(xin[:, t, :], src).then_inc(x_in_s[t], 16)
            pool.wait_ge(pool_start, 1)

            def inverse_root(dst, src, count):
                link(G.tensor_scalar(dst, src, 1.0 / count, EPS, ALU.mult, ALU.add))
                return G.tensor_tensor(dst, dst, neg_half[:, 0:dst.shape[1]], ALU.pow)

            for stage in STAGES:
                kind, a = stage[0], stage[1:]
                if kind == "norm":
                    n = a[0] * NT + a[1]
                    pool.wait_ge(sq_ready, at(*stage))
                    inverse_root(rs_x[:, n:n + 1], ss_x[:, n:n + 1], D).then_inc(rstd_ready, 1)
                elif kind in ("q", "k1", "q1"):
                    n = HEADU[stage]
                    groups = 10 if kind == "q" else 8
                    pool.wait_ge(head_ss, n + 1)
                    if n >= 1:
                        pool.wait_ge(qk_ready, n)
                    inverse_root(rs_h[:, 0:groups], ss_h[:, 0:groups], HD).then_inc(head_rstd, 1)
                elif kind == "ysq":
                    t = a[0]
                    pool.wait_ge(y_sq, t + 1)
                    inverse_root(rs_y[:, t:t + 1], ss_y[:, t:t + 1], B_INNER).then_inc(y_rstd, 1)
                elif kind == "hnorm":
                    h = a[0]
                    pool.wait_ge(o_sq, at("pv1", h, NX - 1))
                    inverse_root(rs_o[:, h * NX:(h + 1) * NX], ss_o[:, h * NX:(h + 1) * NX], C_V).then_inc(o_rstd, 1)
                elif kind == "cb":
                    d, c = a
                    step = STEP[a]
                    if step == 0:
                        pool.wait_ge(tr_done, sum(1 for s in TR if s[0] == "xtr"))
                        wait_done_upto(pool, ("dt", 1))
                        pool.wait_ge(dta_ready, 1)
                    if step >= 2:
                        pool.wait_ge(intra_ready, 4 * (step - 1))
                    x3 = xs[:, c, :].rearrange("p (h d) -> p h d", h=B_HEADS)
                    cut = slice(c * 16, (c + 1) * 16)
                    dt_c = dt_v[:, d * 96:(d + 1) * 96][:, cut].unsqueeze(2).to_broadcast([P, B_HEADS, HD])
                    we = decay[:, (2 * d + 1) * 96:(2 * d + 2) * 96][:, cut].unsqueeze(2).to_broadcast([P, B_HEADS, HD])
                    if d == 1:
                        G.tensor_tensor(yacc[:, c, :].rearrange("p (h d) -> p h d", h=B_HEADS), x3,
                                        dskip.unsqueeze(2).to_broadcast([P, B_HEADS, HD]), ALU.mult)
                    xd = xdt[:, step % 2, :].rearrange("p (h d) -> p h d", h=B_HEADS)
                    G.tensor_tensor(xd, x3, dt_c, ALU.mult).then_inc(xdt_ready, 1)
                    if a not in LAST_STEP:
                        n = STATEU.get(("state",) + STEPS[step - 1] + (1,)) if step else None
                        if n is not None:
                            pool.wait_ge(st_ready, n + 1)
                        pool.wait_ge(xdt_ready, step + 1)
                        G.tensor_tensor(xw.rearrange("p (h d) -> p h d", h=B_HEADS), xd, we, ALU.mult
                                        ).then_inc(xw_ready, 1)
                elif kind == "seg":
                    d, c, q = a
                    n = SEG[stage]
                    if n >= 2:
                        pool.wait_ge(seg_ready, SEGU[SEGS_[n - 2]] + 1)
                    first = d * 96 + c * 16 + 4 * q
                    G.tensor_tensor(tri_v[:, n % 2, :].rearrange("p (h t) -> p h t", h=4),
                                    (le, ge)[d].unsqueeze(1).to_broadcast([P, 4, P]),
                                    dta_v[:, first:first + 4].unsqueeze(2).to_broadcast([P, 4, P]), ALU.mult
                                    ).then_inc(tri_ready, 1)


_INS = ["x", "c", "ctx", "c_ctx", "mod_w", "mod_b", "norm_w", "ev_w_in", "ev_w_out", "ev_q_norm", "ev_k_norm",
        "ev_sink", "ev_conv_w", "ev_conv_b", "ev_dt_bias", "ev_a_log", "ev_d_skip", "ev_ssm_norm", "od_w_in",
        "od_w_out", "od_q_norm", "od_k_norm", "od_lambda", "od_head_norm"]


def kernel(**inputs):
    import numpy as _np
    import concourse.bacc as _bacc
    from concourse import mybir as _mybir
    from concourse.bass_utils import run_bass_kernel_spmd as _run

    nc = _bacc.Bacc("TRN2", target_bir_lowering=False, num_devices=1)
    arrays, aps = {}, {}
    data = {name: _np.ascontiguousarray(inputs[name]) for name in _INS}
    data["tri"] = triangles()
    data["rope"] = rope_tables()
    for name, a in data.items():
        arrays[f"in_{name}_dram"] = a
        aps[name] = nc.dram_tensor(f"in_{name}_dram", a.shape, _mybir.dt.from_np(a.dtype), kind="ExternalInput").ap()
    out = nc.dram_tensor("out_0_dram", (1, SEQ, D), _mybir.dt.float32, kind="ExternalOutput").ap()
    build(nc, aps, out)
    r = _run(nc, [arrays], core_ids=[0])
    return r.results[0]["out_0_dram"]
```
